# Optimizing a Trainium2 kernel written in Bass

```python
import math
import jax, jax.numpy as jnp
from jax import lax
import numpy as np

D_MODEL = 1024
BATCH = 1
SEQ = 128
DEPTH = 2
DEC_BATCH = 1
DEC_SEQ = 256
PAST_LEN = 128

GRID_W = 64
Q_BLOCK = 128
ROPE_BASE = 10000.0
NORM_EPS = 1e-6

DIFF_HEADS = 4
DIFF_QK_DIM = 32
DIFF_V_DIM = 2 * DIFF_QK_DIM
MLA_HEADS = 4
MLA_Q_RANK = 256
MLA_KV_RANK = 128
MLA_NOPE_DIM = 64
MLA_ROPE_DIM = 32
MLA_V_DIM = 64
GQA_HEADS = 8
GQA_KV_HEADS = 2
GQA_HEAD_DIM = 64
GQA_GROUP = GQA_HEADS // GQA_KV_HEADS

MIX_WIDTH = DIFF_HEADS * DIFF_V_DIM + MLA_HEADS * MLA_V_DIM + GQA_HEADS * GQA_HEAD_DIM
IN_SIZES = (DIFF_HEADS * 2 * DIFF_QK_DIM, DIFF_HEADS * 2 * DIFF_QK_DIM, DIFF_HEADS * DIFF_V_DIM,
            MLA_Q_RANK, MLA_KV_RANK, MLA_ROPE_DIM,
            GQA_HEADS * GQA_HEAD_DIM, GQA_KV_HEADS * GQA_HEAD_DIM, GQA_KV_HEADS * GQA_HEAD_DIM)
IN_WIDTH = (3 * DIFF_HEADS * 2 * DIFF_QK_DIM - DIFF_HEADS * 2 * DIFF_QK_DIM + DIFF_HEADS * DIFF_V_DIM
            + MLA_Q_RANK + MLA_KV_RANK + MLA_ROPE_DIM
            + GQA_HEADS * GQA_HEAD_DIM + 2 * GQA_KV_HEADS * GQA_HEAD_DIM)

PEER_HEADS = 8
PEER_N_KEYS = 128
PEER_N_EXPERTS = PEER_N_KEYS * PEER_N_KEYS
PEER_KEY_DIM = 256
PEER_TOPK = 16
PEER_BLOCK = 128

kernel_name = "hybrid_diffusion_peer_trunk_step"

def layer_norm(x, g=None, b=None):
    xf = x.astype(jnp.float32)
    mu = xf.mean(-1, keepdims=True)
    var = jnp.square(xf - mu).mean(-1, keepdims=True)
    y = (xf - mu) * lax.rsqrt(var + NORM_EPS)
    if g is not None:
        y = y * g.astype(jnp.float32) + b.astype(jnp.float32)
    return y.astype(x.dtype)

def rms_norm(x, g):
    xf = x.astype(jnp.float32)
    y = xf * lax.rsqrt(jnp.mean(xf * xf, -1, keepdims=True) + NORM_EPS) * g.astype(jnp.float32)
    return y.astype(x.dtype)

def axial_rope(rows, rot_dim):
    t = jnp.arange(rows * GRID_W)
    row = (t // GRID_W).astype(jnp.float32)
    col = (t % GRID_W).astype(jnp.float32)
    n_freq = rot_dim // 4
    inv = ROPE_BASE ** (-jnp.arange(n_freq, dtype=jnp.float32) / n_freq)
    ang = jnp.concatenate([row[:, None] * inv, col[:, None] * inv], axis=-1)
    return jnp.cos(ang), jnp.sin(ang)

def apply_rope(x, cs):
    cos, sin = cs
    half = x.shape[-1] // 2
    shape = (1, cos.shape[0]) + (1,) * (x.ndim - 3) + (half,)
    c = cos.reshape(shape)
    s = sin.reshape(shape)
    x1, x2 = x[..., :half], x[..., half:]
    return jnp.concatenate([x1 * c - x2 * s, x1 * s + x2 * c], axis=-1).astype(x.dtype)

def sweep_queries(fn, *qs):
    B, S = qs[0].shape[:2]
    nb = S // Q_BLOCK
    blocks = tuple(jnp.moveaxis(q.reshape((B, nb, Q_BLOCK) + q.shape[2:]), 1, 0) for q in qs)
    out = lax.map(lambda blk: fn(*blk), blocks)
    out = jnp.moveaxis(out, 0, 1)
    return out.reshape((B, S) + out.shape[3:])

def mixers(h, rope, ctx, lp, lambda_init):
    B, S, _ = h.shape
    proj = h @ lp['w_in']
    offs, acc = [], 0
    for sz in IN_SIZES[:-1]:
        acc += sz
        offs.append(acc)
    a_q, a_k, a_v, m_cq, m_ckv, m_kr, g_q, g_k, g_v = jnp.split(proj, offs, axis=-1)

    a_q = a_q.reshape(B, S, DIFF_HEADS, 2, DIFF_QK_DIM)
    a_k = a_k.reshape(B, S, DIFF_HEADS, 2, DIFF_QK_DIM)
    a_v = a_v.reshape(B, S, DIFF_HEADS, DIFF_V_DIM)
    q_mla = (rms_norm(m_cq, lp['mla_q_norm_g']) @ lp['mla_w_uq']).reshape(
        B, S, MLA_HEADS, MLA_NOPE_DIM + MLA_ROPE_DIM)
    q_nope, q_rope = q_mla[..., :MLA_NOPE_DIM], q_mla[..., MLA_NOPE_DIM:]
    m_ckv = rms_norm(m_ckv, lp['mla_kv_norm_g'])
    g_q = rms_norm(g_q.reshape(B, S, GQA_HEADS, GQA_HEAD_DIM), lp['gqa_q_norm_g'])
    g_k = rms_norm(g_k.reshape(B, S, GQA_KV_HEADS, GQA_HEAD_DIM), lp['gqa_k_norm_g'])
    g_v = g_v.reshape(B, S, GQA_KV_HEADS, GQA_HEAD_DIM)
    own_ctx = (a_k, a_v, m_ckv, m_kr, g_k, g_v)

    if ctx is None:
        keys = own_ctx
    else:
        rope_diff, rope_mla, rope_gqa = rope
        a_q = apply_rope(a_q, rope_diff)
        q_rope = apply_rope(q_rope, rope_mla)
        g_q = apply_rope(g_q, rope_gqa)
        own = (apply_rope(a_k, rope_diff), a_v, m_ckv, apply_rope(m_kr, rope_mla),
               apply_rope(g_k, rope_gqa), g_v)
        keys = tuple(jnp.concatenate([o, cc], axis=1) for o, cc in zip(own, ctx))
    k_a, v_a, ckv_all, kr_all, k_g, v_g = keys
    K = k_a.shape[1]

    dl = lp['diff_lambda'].astype(jnp.float32)
    lam = jnp.exp(jnp.sum(dl[0] * dl[1])) - jnp.exp(jnp.sum(dl[2] * dl[3])) + lambda_init
    scale_a = DIFF_QK_DIM ** -0.5

    def diff_block(qb):
        s = jnp.einsum('bqhcd,bkhcd->bhcqk', qb, k_a).astype(jnp.float32) * scale_a
        p = jax.nn.softmax(s, axis=-1)
        p = p[:, :, 0] - lam * p[:, :, 1]
        return jnp.einsum('bhqk,bkhe->bqhe', p.astype(v_a.dtype), v_a)

    out_a = sweep_queries(diff_block, a_q)
    out_a = (rms_norm(out_a, lp['diff_subln_g']) * (1.0 - lambda_init)).reshape(B, S, DIFF_HEADS * DIFF_V_DIM)

    kv = (ckv_all @ lp['mla_w_ukv']).reshape(B, K, MLA_HEADS, MLA_NOPE_DIM + MLA_V_DIM)
    k_nope, v_m = kv[..., :MLA_NOPE_DIM], kv[..., MLA_NOPE_DIM:]
    scale_b = (MLA_NOPE_DIM + MLA_ROPE_DIM) ** -0.5

    def mla_block(qn, qr):
        s = (jnp.einsum('bqhd,bkhd->bhqk', qn, k_nope)
             + jnp.einsum('bqhr,bkr->bhqk', qr, kr_all)).astype(jnp.float32) * scale_b
        p = jax.nn.softmax(s, axis=-1)
        return jnp.einsum('bhqk,bkhe->bqhe', p.astype(v_m.dtype), v_m)

    out_b = sweep_queries(mla_block, q_nope, q_rope).reshape(B, S, MLA_HEADS * MLA_V_DIM)

    scale_c = GQA_HEAD_DIM ** -0.5
    g_q = g_q.reshape(B, S, GQA_KV_HEADS, GQA_GROUP, GQA_HEAD_DIM)

    def gqa_block(qb):
        s = jnp.einsum('bqhgd,bkhd->bhgqk', qb, k_g).astype(jnp.float32) * scale_c
        p = jax.nn.softmax(s, axis=-1)
        return jnp.einsum('bhgqk,bkhd->bqhgd', p.astype(v_g.dtype), v_g)

    out_c = sweep_queries(gqa_block, g_q).reshape(B, S, GQA_HEADS * GQA_HEAD_DIM)

    mix = jnp.concatenate([out_a, out_b, out_c], axis=-1) @ lp['w_out']
    return mix, own_ctx

def peer_ffn(h, wq, keys, u_tab, v_tab):
    B, S, D = h.shape
    half = PEER_KEY_DIM // 2
    q = (h @ wq).reshape(B, S, PEER_HEADS, 2, half)
    s = jnp.einsum('bshcd,hckd->bshck', q, keys).astype(jnp.float32)
    s_top, i_top = lax.top_k(s, PEER_TOPK)
    cand = (s_top[..., 0, :, None] + s_top[..., 1, None, :]).reshape(B, S, PEER_HEADS, PEER_TOPK * PEER_TOPK)
    best_s, best_i = lax.top_k(cand, PEER_TOPK)
    e1 = jnp.take_along_axis(i_top[..., 0, :], best_i // PEER_TOPK, axis=-1)
    e2 = jnp.take_along_axis(i_top[..., 1, :], best_i % PEER_TOPK, axis=-1)
    experts = e1 * PEER_N_KEYS + e2
    gates = jax.nn.softmax(best_s, axis=-1).astype(h.dtype)
    nb = (B * S) // PEER_BLOCK
    xf = h.reshape(nb, PEER_BLOCK, D)
    ef = experts.reshape(nb, PEER_BLOCK, PEER_HEADS * PEER_TOPK)
    gf = gates.reshape(nb, PEER_BLOCK, PEER_HEADS * PEER_TOPK)

    def block(args):
        xb, eb, gb = args
        u = jnp.take(u_tab, eb, axis=0)
        act = jax.nn.gelu(jnp.einsum('td,tkd->tk', xb, u))
        return jnp.einsum('tk,tkd->td', gb * act, jnp.take(v_tab, eb, axis=0))

    return lax.map(block, (xf, ef, gf)).reshape(B, S, D)

def trunk_layer(x, cond, rope, ctx, lp, lambda_init, alpha):
    mod = jax.nn.silu(cond) @ lp['w_mod'] + lp['b_mod']
    sh1, sc1, g1, sh2, sc2, g2 = jnp.split(mod[:, None, :], 6, axis=-1)
    h = layer_norm(x) * (1.0 + sc1) + sh1
    mix, own_ctx = mixers(h, rope, ctx, lp, lambda_init)
    x = layer_norm(alpha * x + g1 * mix, lp['ln1_g'], lp['ln1_b'])
    h = layer_norm(x) * (1.0 + sc2) + sh2
    ff = peer_ffn(h, lp['peer_wq'], lp['peer_keys'], lp['peer_u'], lp['peer_v'])
    x = layer_norm(alpha * x + g2 * ff, lp['ln2_g'], lp['ln2_b'])
    return x, own_ctx

def setup_inputs(seed: int = 0) -> dict:
    key = jax.random.key(seed)
    ks = jax.random.split(key, 40)

    def nrm(k, shape, scale):
        return jax.random.normal(k, shape, jnp.float32) * scale

    out_scale = (8 * DEPTH) ** -0.25
    L, T, Bd = DEPTH, PAST_LEN, DEC_BATCH
    return {
        'x_prompt': nrm(ks[0], (BATCH, SEQ, D_MODEL), 1.0),
        'x_sample': nrm(ks[1], (DEC_BATCH, DEC_SEQ, D_MODEL), 1.0),
        'c': nrm(ks[2], (DEC_BATCH, D_MODEL), 1.0),
        'cache_diff_k': nrm(ks[3], (Bd, L, T, DIFF_HEADS, 2, DIFF_QK_DIM), 1.0),
        'cache_diff_v': nrm(ks[4], (Bd, L, T, DIFF_HEADS, DIFF_V_DIM), 1.0),
        'cache_mla_ckv': nrm(ks[5], (Bd, L, T, MLA_KV_RANK), 1.0),
        'cache_mla_krope': nrm(ks[6], (Bd, L, T, MLA_ROPE_DIM), 1.0),
        'cache_gqa_k': nrm(ks[7], (Bd, L, T, GQA_KV_HEADS, GQA_HEAD_DIM), 1.0),
        'cache_gqa_v': nrm(ks[8], (Bd, L, T, GQA_KV_HEADS, GQA_HEAD_DIM), 1.0),
        'c_ctx': nrm(ks[9], (D_MODEL,), 1.0),
        'w_mod': nrm(ks[10], (L, D_MODEL, 6 * D_MODEL), 0.5 * D_MODEL ** -0.5),
        'b_mod': nrm(ks[11], (L, 6 * D_MODEL), 0.02),
        'w_in': nrm(ks[12], (L, D_MODEL, IN_WIDTH), D_MODEL ** -0.5),
        'diff_lambda': nrm(ks[13], (L, 4, DIFF_QK_DIM), 0.1),
        'diff_subln_g': 1.0 + nrm(ks[14], (L, DIFF_V_DIM), 0.02),
        'mla_q_norm_g': 1.0 + nrm(ks[15], (L, MLA_Q_RANK), 0.02),
        'mla_kv_norm_g': 1.0 + nrm(ks[16], (L, MLA_KV_RANK), 0.02),
        'mla_w_uq': nrm(ks[17], (L, MLA_Q_RANK, MLA_HEADS * (MLA_NOPE_DIM + MLA_ROPE_DIM)), MLA_Q_RANK ** -0.5),
        'mla_w_ukv': nrm(ks[18], (L, MLA_KV_RANK, MLA_HEADS * (MLA_NOPE_DIM + MLA_V_DIM)), MLA_KV_RANK ** -0.5),
        'gqa_q_norm_g': 1.0 + nrm(ks[19], (L, GQA_HEAD_DIM), 0.02),
        'gqa_k_norm_g': 1.0 + nrm(ks[20], (L, GQA_HEAD_DIM), 0.02),
        'w_out': nrm(ks[21], (L, MIX_WIDTH, D_MODEL), MIX_WIDTH ** -0.5 * out_scale),
        'ln1_g': 1.0 + nrm(ks[22], (L, D_MODEL), 0.02),
        'ln1_b': nrm(ks[23], (L, D_MODEL), 0.02),
        'ln2_g': 1.0 + nrm(ks[24], (L, D_MODEL), 0.02),
        'ln2_b': nrm(ks[25], (L, D_MODEL), 0.02),
        'peer_wq': nrm(ks[26], (L, D_MODEL, PEER_HEADS * PEER_KEY_DIM), D_MODEL ** -0.5),
        'peer_keys': nrm(ks[27], (L, PEER_HEADS, 2, PEER_N_KEYS, PEER_KEY_DIM // 2), (PEER_KEY_DIM // 2) ** -0.5),
        'peer_u': nrm(ks[28], (L, PEER_N_EXPERTS, D_MODEL), D_MODEL ** -0.5),
        'peer_v': nrm(ks[29], (L, PEER_N_EXPERTS, D_MODEL), out_scale),
    }

def reference(x_prompt, x_sample, c, cache_diff_k, cache_diff_v, cache_mla_ckv, cache_mla_krope,
              cache_gqa_k, cache_gqa_v, c_ctx, w_mod, b_mod, w_in, diff_lambda, diff_subln_g,
              mla_q_norm_g, mla_kv_norm_g, mla_w_uq, mla_w_ukv, gqa_q_norm_g, gqa_k_norm_g, w_out,
              ln1_g, ln1_b, ln2_g, ln2_b, peer_wq, peer_keys, peer_u, peer_v):
    alpha = (2 * DEPTH) ** 0.25
    rows = x_sample.shape[1] // GRID_W
    rope = (axial_rope(rows, DIFF_QK_DIM), axial_rope(rows, MLA_ROPE_DIM), axial_rope(rows, GQA_HEAD_DIM))
    ctx_cond = c_ctx[None, :]
    yp, ys = x_prompt, x_sample
    new = [[], [], [], [], [], []]
    for l in range(DEPTH):
        lp = dict(w_mod=w_mod[l], b_mod=b_mod[l], w_in=w_in[l], diff_lambda=diff_lambda[l],
                  diff_subln_g=diff_subln_g[l], mla_q_norm_g=mla_q_norm_g[l], mla_kv_norm_g=mla_kv_norm_g[l],
                  mla_w_uq=mla_w_uq[l], mla_w_ukv=mla_w_ukv[l], gqa_q_norm_g=gqa_q_norm_g[l],
                  gqa_k_norm_g=gqa_k_norm_g[l], w_out=w_out[l], ln1_g=ln1_g[l], ln1_b=ln1_b[l],
                  ln2_g=ln2_g[l], ln2_b=ln2_b[l], peer_wq=peer_wq[l], peer_keys=peer_keys[l],
                  peer_u=peer_u[l], peer_v=peer_v[l])
        lambda_init = 0.8 - 0.6 * math.exp(-0.3 * l)
        yp, ctx_l = trunk_layer(yp, ctx_cond, None, None, lp, lambda_init, alpha)
        for lst, t in zip(new, ctx_l):
            lst.append(t)
        cached = (cache_diff_k[:, l], cache_diff_v[:, l], cache_mla_ckv[:, l], cache_mla_krope[:, l],
                  cache_gqa_k[:, l], cache_gqa_v[:, l])
        ys, _ = trunk_layer(ys, c, rope, cached, lp, lambda_init, alpha)
    new_diff_k = jnp.stack(new[0], axis=1)
    new_diff_v = jnp.stack(new[1], axis=1)
    new_mla_ckv = jnp.stack(new[2], axis=1)
    new_mla_krope = jnp.stack(new[3], axis=1)
    new_gqa_k = jnp.stack(new[4], axis=1)
    new_gqa_v = jnp.stack(new[5], axis=1)
    return (yp, ys, new_diff_k, new_diff_v, new_mla_ckv, new_mla_krope, new_gqa_k, new_gqa_v)


_drawn_inputs = setup_inputs


def setup_inputs(seed=0):
    import zlib

    import numpy as np

    out = dict(_drawn_inputs(seed))
    spreads = {}
    factors = {'cache_diff_k': 3.25,
     'cache_diff_v': 2.993,
     'cache_mla_ckv': 8.0,
     'cache_mla_krope': 8.0,
     'cache_gqa_k': 7.944,
     'cache_gqa_v': 6.623,
     'diff_lambda': 8.0,
     'diff_subln_g': 8.0,
     'mla_q_norm_g': 8.0,
     'mla_kv_norm_g': 2.738,
     'mla_w_uq': 4.944,
     'gqa_q_norm_g': 8.0,
     'gqa_k_norm_g': 8.459}
    for name, (base, spread) in spreads.items():
        noise = np.random.default_rng([zlib.crc32(name.encode()), seed]).standard_normal(out[name].shape)
        drawn = base * np.exp(spread * noise) if base else spread * noise
        out[name] = __import__('jax').numpy.asarray(drawn.astype(out[name].dtype))
    for name, factor in factors.items():
        out[name] = (out[name] * factor).astype(out[name].dtype)
    return out
```

```python
import math
from contextlib import ExitStack

import concourse.bass as bass
from concourse import mybir

F32 = mybir.dt.float32
I32 = mybir.dt.int32
U32 = mybir.dt.uint32
ALU = mybir.AluOpType
ACT = mybir.ActivationFunctionType
X = mybir.AxisListType.X

P = 128
D = 1024
KT = D // P
L = 2
PAST = 128
GRID_W = 64
EPS = 1e-6
ALPHA = (2 * L) ** 0.25
N_EXP = 128 * 128
TOPK = 16
R_HEADS = 8
SLOTS = R_HEADS * TOPK
AQ, AK, AV, CQ, CKV, KR, GQ, GK, GV, WIN = 0, 256, 512, 768, 1024, 1152, 1184, 1696, 1824, 1952
CA_K, CA_V, CA_CKV, CA_KR, CA_GK, CA_GV, CA_N = 0, 256, 512, 640, 672, 800, 928
G_Q, G_K, G_SUB, G_KV, G_CQ, G_N = 0, 64, 128, 192, 320, 576
WT = 2048
IN_T = 8
IN_C = WIN // IN_T
OUT_T = 4
WQ_T = 8
MOD_T = 4
UQ_N = 384
UKV_N = 512
MATS = 20
PER_STEP = 4
SCALE = [32 ** -0.5] * 8 + [96 ** -0.5] * 4 + [64 ** -0.5] * 8
AREA = 8448
RING = 6
WRING = 3

BLOCKS = {"P": (0,), "S": (1, 2)}
KEYS = {"P": 1, "S": 3}


def lambda_init(l):
    return 0.8 - 0.6 * math.exp(-0.3 * l)


COST = {"mod": 16, "ln1": 5, "win": 3, "prep": 12, "prep_t": 9, "q_rope": 2, "qm_t": 2, "cache_t": 3,
        "kv_mla": 6, "heads": 9, "mix": 4, "mix_t": 3, "wout": 3, "ln_x": 7, "ln_h": 4, "h_t": 3,
        "wq": 4, "r_score": 2, "topk": 5, "pick": 12, "fin": 8}
WEIGHTED = ("win", "wout", "wq", "mod", "kv_mla")


def attention_steps(l, s):
    B = BLOCKS[s]
    out = []
    for b in B:
        out += [("ln1", l, s, b, 0), ("h_t", l, s, b, 0)]
    out += [("win", l, s, n, 0) for n in range(IN_T)]
    for b in B:
        out += [("prep", l, s, b, 0), ("prep_t", l, s, b, 0), ("q_rope", l, s, b, 0), ("qm_t", l, s, b, 0)]
    if s == "S":
        out += [("cache_t", l, s, 0, 0)]
    out += [("kv_mla", l, s, 0, 0)]
    for b in B:
        out += [("heads", l, s, b, i) for i in range(MATS // PER_STEP)]
        out += [("mix", l, s, b, 0), ("h_t", l, s, b, 1)]
    out += [("wout", l, s, n, 0) for n in range(OUT_T)]
    out += [("ln_x", l, s, b, 0) for b in B]
    for b in B:
        out += [("ln_h", l, s, b, 0), ("h_t", l, s, b, 2)]
    out += [("wq", l, s, n, 0) for n in range(WQ_T)]
    for b in B:
        out += [("r_score", l, s, b, q) for q in range(4)]
        out += [("topk", l, s, b, h) for h in range(R_HEADS)]
        out += [("pick", l, s, b, c) for c in range(2)]
    return out


def mod_steps(l):
    return [("mod", l, "", row, 0) for row in range(6)]


def weave(slots, steps):
    total = sum(COST[x[0]] for x in steps) or 1
    todo = [(l, b, k) for l, b in slots for k in range(SLOTS)]
    out, done, cost = [], 0, 0

    def run(upto):
        nonlocal done
        while done < upto:
            l, b, k = todo[done]
            n = min(upto - done, SLOTS - k)
            out.append(("peer", l, "", b, (k, n)))
            done += n
            if k + n == SLOTS:
                out.append(("fin", l, "", b, 0))

    for x in steps:
        out.append(x)
        cost += COST[x[0]]
        at = (len(todo) * cost // total) // RING * RING
        if at - done >= RING:
            run(at)
    run(len(todo))
    return out


def plan():
    steps = [("cond", 0, "", 0, 0)] + mod_steps(0) + attention_steps(0, "P")
    steps += weave([(0, 0)], attention_steps(0, "S"))
    steps += weave([(0, 1), (0, 2)], mod_steps(1) + attention_steps(1, "P"))
    steps += weave([(1, 0)], attention_steps(1, "S"))
    steps += weave([(1, 1), (1, 2)], [])
    return steps


STEPS = plan()


def banks_used(x):
    kind, l, s, i, e = x
    return {"cond": (0, 1), "mod": (MOD_T, 0), "h_t": (0, 2), "win": (1, 0), "prep_t": (1, 4), "qm_t": (0, 1),
            "cache_t": (0, 2), "kv_mla": (4 + KEYS.get(s, 0), 0), "heads": (PER_STEP, PER_STEP),
            "wout": (1, 0), "wq": (1, 0), "r_score": (1, 0)}.get(kind, (0, 0))


def walk():
    mm = t = slot = 0
    for x in STEPS:
        yield x, mm, t, slot
        a, b = banks_used(x)
        mm, t = mm + a, t + b
        if x[0] == "peer":
            slot += x[4][1]


def row_groups():
    out = []
    for kind, l, s, i, e in STEPS:
        if kind == "fin":
            out.append((l, "P" if i == 0 else "S", "g2"))
        name = {"ln1": "sh1", "ln_x": "g1", "ln_h": "sh2"}.get(kind)
        if name and (l, s, name) not in out:
            out.append((l, s, name))
    return out


def slot_runs(k, n, peel):
    out = []
    if peel:
        out.append((0, 1, 1))
        k, n = k + 1, n - 1
    if n // RING >= 2:
        out.append((k, n // RING, RING))
        k, n = k + n // RING * RING, n % RING
    while n:
        m = min(n, RING)
        out.append((k, 1, m))
        k, n = k + m, n - m
    return out


def trunk_program(nc, t_in, t_out):
    with ExitStack() as ctx:
        def sb(name, shape, dt=F32):
            return ctx.enter_context(nc.sbuf_tensor(name, shape, dt))

        def ps(name, shape):
            return ctx.enter_context(nc.psum_tensor(name, shape, F32))

        def sem(name):
            return ctx.enter_context(nc.semaphore(name))

        expert = sb("expert", [P, RING, 2 * D])
        wt = sb("wt", [P, WRING, WT])
        rows = sb("rows", [P, 2, 3, D])
        x = sb("x", [P, 3, D])
        h2 = sb("h2", [P, 3, D])
        hT = sb("hT", [P, KT, 2 * P])
        wide = sb("wide", [P, 4096])
        tok = sb("tok", [P, D])
        tmp = sb("tmp", [P, 1280])
        area = sb("area", [P, AREA])
        cache = sb("cache", [P, CA_N])
        ident = sb("ident", [P, P])
        iota = sb("iota", [P, TOPK])
        rope = sb("rope", [P, 2, 192])
        gain = sb("gain", [P, L, G_N])
        neglam = sb("neglam", [P, L])
        small = sb("small", [P, 64])
        newton = sb("newton", [P, 20])
        neg_max = sb("neg_max", [P, MATS])
        row_sum = sb("row_sum", [P, MATS])
        csT = sb("csT", [P, 2, KT])
        i16 = sb("i16", [P, 16, TOPK], U32)
        bi = sb("bi", [P, R_HEADS, TOPK], U32)
        bit = sb("bit", [P, SLOTS], U32)
        eidx = sb("eidx", [P, 3, SLOTS], I32)
        gate = sb("gate", [P, 3, SLOTS])
        dots = sb("dots", [P, RING])
        acts = sb("acts", [P, RING])
        diag = sb("diag", [P, RING, P])
        mod_dram = nc.dram_tensor("mod_scratch", (L, 2, 6, D), F32, kind="Internal").ap()

        acc = ps("acc", [P, D])
        mmb = [ps(f"mmb{i}", [P, 512]) for i in range(2)]
        trb = [ps(f"trb{i}", [P, 512]) for i in range(2)]
        ob = [ps(f"ob{i}", [P, 512]) for i in range(2)]

        def cut(t, at, shape):
            n = int(math.prod(shape))
            v = t[:, at:at + n]
            if len(shape) == 2:
                v = v.rearrange("p (a b) -> p a b", b=shape[1])
            if len(shape) == 3:
                v = v.rearrange("p (a b c) -> p a b c", b=shape[1], c=shape[2])
            return v

        def proj(b):
            j = max(b - 1, 0)
            return wide[:, j * WIN:(j + 1) * WIN]

        def ymix(b):
            j = max(b - 1, 0)
            return wide[:, j * D:(j + 1) * D]

        qT = cut(wide, 0, (16, 2 * P))
        mrow = cut(wide, 0, (2, D))
        brow = cut(wide, 2 * D, (2, D))
        at = 0
        views = {}
        for name, shape in (("qdT", (2, 256)), ("qgT", (4, 256)), ("qmT", (4, 256)), ("kdT", (2, 384)),
                            ("kgT", (384,)), ("kmT", (4, 384)), ("ckvT", (384,)), ("vm", (3, 256)),
                            ("E", (2, 384)), ("ET", (2, 384)), ("od", (512,))):
            views[name] = cut(area, at, shape)
            at += int(math.prod(shape))
        assert at <= AREA, at
        qdT, qgT, qmT, kdT, kgT, kmT, ckvT, vm, E, ET, od = views.values()
        at_vm = 512 + 1024 + 1024 + 768 + 384 + 1536 + 384
        qm = cut(area, at_vm, (UQ_N,))
        cqT = cut(area, at_vm + UQ_N, (2, 128))
        at = 0
        views = {}
        for name, shape in (("rs", (16, 128)), ("rep", (128,)), ("cand", (16, 16)), ("cand2", (256,)),
                            ("eq", (R_HEADS, TOPK, 16)), ("v16", (16, TOPK)), ("i16f", (R_HEADS, 2, TOPK)),
                            ("best", (R_HEADS, TOPK)), ("bf", (SLOTS,)), ("e1", (SLOTS,)), ("e2", (SLOTS,))):
            views[name] = cut(area, at, shape)
            at += int(math.prod(shape))
        assert at <= AREA, at
        rs, rep, cand, cand2, eq, v16, i16f, best, bf, e1, e2 = views.values()
        dlam = cut(area, 0, (L, P))
        cond_rows = area[0:2 * KT, L * P:L * P + P]
        cond_e = area[0:2 * KT, L * P + P:L * P + 2 * P]
        t1, t2 = tmp[:, 0:640], tmp[:, 640:1280]

        const_in = sem("const_in")
        cache_in = sem("cache_in")
        w_in_slot = [sem(f"w_in_slot{i}") for i in range(WRING)]
        rows_in = [sem(f"rows_in{i}") for i in range(2)]
        rows_used = sem("rows_used")
        bias_in = [sem(f"bias_in{i}") for i in range(2)]
        mod_row = sem("mod_row")
        mod_stored = [sem(f"mod_stored{i}") for i in range(6)]
        mm_full = sem("mm_full")
        mm_free = sem("mm_free")
        t_full = sem("t_full")
        t_free = sem("t_free")
        sc_full = sem("sc_full")
        nmax_ready = sem("nmax_ready")
        o_full = sem("o_full")
        o_free = sem("o_free")
        lam_dots = sem("lam_dots")
        lam_exp = sem("lam_exp")
        cond_exp = sem("cond_exp")
        cond_silu = sem("cond_silu")
        tok_ready = sem("tok_ready")
        h2_ready = sem("h2_ready")
        prep_done = sem("prep_done")
        roped = sem("roped")
        kv_stored = sem("kv_stored")
        gate_diff = sem("gate_diff")
        gate_exp = sem("gate_exp")
        idx_ready = sem("idx_ready")
        landed = [sem(f"landed{i}") for i in range(RING)]
        dot_ready = sem("dot_ready")
        act_ready = sem("act_ready")
        diag_ready = sem("diag_ready")
        slot_done = sem("slot_done")
        acc_read = sem("acc_read")
        y_ready = sem("y_ready")
        y_stored = sem("y_stored")
        v_seq = sem("v_seq")
        a_seq = sem("a_seq")

        def counter():
            seen = {}

            def count(name, n=1):
                seen[name] = seen.get(name, 0) + n
                return seen[name]
            return count

        tiles, router_end = [], {}
        for (kind, l, s, i, e), mm, _, _ in walk():
            if kind == "mod":
                tiles += [["mod", l, MOD_T * i + c, mm + c + 1] for c in range(MOD_T)]
            if kind in ("win", "wout", "wq"):
                tiles.append([kind, l, i, mm + 1])
            if kind == "prep_t" and i == BLOCKS[s][0]:
                small_tile = ["small", l, 0, 0]
                tiles.append(small_tile)
            if kind == "kv_mla":
                small_tile[3] = mm + 4 + KEYS[s]
            if kind == "r_score":
                if i == BLOCKS[s][0] and e == 0:
                    keys_tile = ["keys", l, 0, 0]
                    tiles.append(keys_tile)
                keys_tile[3] = router_end[l, s] = mm + 1
        GROUPS = row_groups()

        block = ctx.enter_context(nc.Block())

        @block.sync
        def _(sp):
            n_const = counter()
            for dst, src in ((ident[:], t_in["ident"]), (cond_rows, t_in["cond"]), (iota[:], t_in["iota"]),
                             (rope[:], t_in["rope"]), (gain[:], t_in["gain"].partition_broadcast(P)),
                             (dlam, t_in["dlam"].partition_broadcast(P)),
                             (x[:, 0, :], t_in["x_prompt"]), (x[:, 1, :], t_in["x_sample"][0:P, :]),
                             (x[:, 2, :], t_in["x_sample"][P:2 * P, :])):
                sp.dma_start(dst, src).then_inc(const_in, 16)
                n_const("c")
            assert n_const("c", 0) == N_CONST
            tile = 0
            group = 0

            def load_tile():
                nonlocal tile
                kind, l, i, _ = tiles[tile]
                if tile >= WRING:
                    sp.wait_ge(mm_free, tiles[tile - WRING][3])
                src = t_in["w_" + kind][l, i]
                n = src.shape[-1]
                sp.dma_start(wt[:, tile % WRING, 0:n], src).then_inc(w_in_slot[tile % WRING], 16)
                tile += 1

            def load_rows():
                nonlocal group
                l, s, name = GROUPS[group]
                if group >= 2:
                    sp.wait_ge(rows_used, group - 1)
                first = {"sh1": 0, "g1": 2, "sh2": 3, "g2": 5}[name]
                many = 2 if name in ("sh1", "sh2") else 1
                for r in range(first, first + many):
                    sp.wait_ge(mod_stored[r], 16 * (l + 1))
                j = {"P": 0, "S": 1}[s]
                buf = group % 2
                sp.dma_start(rows[:, buf, 0:many, :],
                             mod_dram[l, j, first:first + many, :].partition_broadcast(P)).then_inc(rows_in[buf], 16)
                if many == 1:
                    sp.dma_start(rows[:, buf, 1:3, :],
                                 t_in["ln"][l, 0 if name == "g1" else 1].partition_broadcast(P)).then_inc(rows_in[buf], 16)
                group += 1

            seen_rows = []
            biases = 0
            for kind, l, s, i, e in STEPS:
                if kind == "mod":
                    if l > 0 and i == 0:
                        sp.wait_ge(mm_free, router_end[l - 1, "S"])
                    if biases >= 2:
                        sp.wait_ge(mod_row, biases - 1)
                    sp.dma_start(brow[0:2, biases % 2, :],
                                 t_in["b_mod"][l, i].partition_broadcast(2)).then_inc(bias_in[biases % 2], 16)
                    biases += 1
                    for c in range(MOD_T):
                        load_tile()
                name = {"ln1": "sh1", "ln_x": "g1", "ln_h": "sh2"}.get(kind)
                if kind == "fin":
                    load_rows()
                elif name and (l, s, name) not in seen_rows:
                    seen_rows.append((l, s, name))
                    load_rows()
                if kind in ("win", "wout", "wq"):
                    load_tile()
                if kind == "prep_t" and i == BLOCKS[s][0]:
                    load_tile()
                if kind == "r_score" and i == BLOCKS[s][0] and e == 0:
                    load_tile()
                if kind == "win" and i == 0 and s == "S":
                    if l > 0:
                        sp.wait_ge(mm_free, router_end[l - 1, "S"])
                    sp.dma_start(cache[:], t_in["cache"][l]).then_inc(cache_in, 16)
            ys = 0
            for b, dst in ((0, t_out["y_prompt"]), (1, t_out["y_sample"][0:P, :]), (2, t_out["y_sample"][P:2 * P, :])):
                ys += 1
                sp.wait_ge(y_ready, ys)
                sp.dma_start(dst, x[:, b, :]).then_inc(y_stored, 16)
            sp.wait_ge(y_stored, 16 * ys)

        @block.gpsimd
        def _(pool):
            blocks_seen = 0
            for (kind, l, s, b, e), mm, t, slot in walk():
                if kind != "peer":
                    continue
                k0, n = e
                if k0 == 0:
                    blocks_seen += 1
                    pool.wait_ge(idx_ready, blocks_seen)
                for k in range(k0, k0 + n):
                    g = slot + k - k0
                    if g >= RING:
                        pool.wait_ge(slot_done, g - RING + 1)
                    pool.indirect_dma_start(expert[:, g % RING, :], None, t_in["experts"],
                                            bass.IndirectOffsetOnAxis(eidx[:, b, k:k + 1], 0)
                                            ).then_inc(landed[g % RING], 16)

        @block.tensor
        def _(pe):
            n = counter()
            tile = 0

            def mm_bank(u):
                if u >= 2:
                    pe.wait_ge(mm_free, u - 1)
                return mmb[u % 2]

            def t_bank(u):
                if u >= 2:
                    pe.wait_ge(t_free, u - 1)
                return trb[u % 2]

            def weights():
                nonlocal tile
                pe.wait_ge(w_in_slot[tile % WRING], 16 * (tile // WRING + 1))
                tile += 1
                return wt[:, (tile - 1) % WRING, :]

            for (kind, l, s, b, e), mm, t, slot in walk():
                B = BLOCKS.get(s, ())
                NB, KB = len(B), KEYS.get(s, 0)
                K = KB * P
                j = max(b - 1, 0)
                cols = slice(j * P, (j + 1) * P)

                if kind == "cond":
                    pe.wait_ge(cond_silu, 1)
                    pe.transpose(t_bank(t)[:, 0:16], cond_rows, ident[0:16, 0:16]).then_inc(t_full, 1)

                if kind == "mod":
                    if l == 0 and b == 0:
                        pe.wait_ge(t_free, 1)
                    for c in range(MOD_T):
                        bank = mm_bank(mm + c)
                        w = weights()
                        for kt in range(KT):
                            m = pe.matmul(bank[0:2, 0:256], csT[:, :, kt], w[:, kt * 256:(kt + 1) * 256],
                                          start=kt == 0, stop=kt == KT - 1)
                        m.then_inc(mm_full, 1)

                if kind == "h_t":
                    if e == 2:
                        pe.wait_ge(h2_ready, n("h2"))
                        src = h2[:, b, :]
                    else:
                        pe.wait_ge(tok_ready, n("tok"))
                        src = tok[:]
                    for half in range(2):
                        bank = t_bank(t + half)
                        for q in range(4):
                            c = 4 * half + q
                            m = pe.transpose(bank[:, q * P:(q + 1) * P], src[:, c * P:(c + 1) * P], ident[:])
                        m.then_inc(t_full, 1)

                if kind in ("win", "wout"):
                    width = IN_C if kind == "win" else 256
                    if b == 0:
                        pe.wait_ge(t_free, t)
                    bank = mm_bank(mm)
                    w = weights()
                    for jj in range(NB):
                        for kt in range(KT):
                            m = pe.matmul(bank[:, jj * 256:jj * 256 + width], hT[:, kt, jj * P:(jj + 1) * P],
                                          w[:, kt * width:(kt + 1) * width], start=kt == 0, stop=kt == KT - 1)
                    m.then_inc(mm_full, 1)

                if kind == "wq":
                    if b == 0:
                        pe.wait_ge(t_free, t)
                    bank = mm_bank(mm)
                    w = weights()
                    for i in range(2):
                        for kt in range(KT):
                            m = pe.matmul(bank[:, i * 256:i * 256 + NB * P],
                                          w[:, kt * 256 + i * P:kt * 256 + (i + 1) * P], hT[:, kt, 0:NB * P],
                                          start=kt == 0, stop=kt == KT - 1)
                    m.then_inc(mm_full, 1)

                if kind == "prep_t":
                    pe.wait_ge(prep_done, n("prep"))
                    p = proj(b)
                    bank = t_bank(t)
                    for q, c in enumerate((AQ, AQ + P, AK, AK + P)):
                        m = pe.transpose(bank[:, q * P:(q + 1) * P], p[:, c:c + P], ident[:])
                    m.then_inc(t_full, 1)
                    bank = t_bank(t + 1)
                    for q in range(4):
                        m = pe.transpose(bank[:, q * P:(q + 1) * P], p[:, GQ + q * P:GQ + (q + 1) * P], ident[:])
                    m.then_inc(t_full, 1)
                    bank = t_bank(t + 2)
                    pe.transpose(bank[:, 0:P], p[:, GK:GV], ident[:])
                    pe.transpose(bank[:, P:2 * P], p[:, CKV:KR], ident[:])
                    pe.transpose(bank[0:96, 2 * P:3 * P], p[:, KR - 64:GQ], ident[:]).then_inc(t_full, 1)
                    bank = t_bank(t + 3)
                    pe.transpose(bank[:, 0:P], p[:, CQ:CQ + P], ident[:])
                    pe.transpose(bank[:, P:2 * P], p[:, CQ + P:CKV], ident[:]).then_inc(t_full, 1)
                    if b == B[0]:
                        small_w = weights()
                    pe.wait_ge(t_free, t + 4)
                    bank = mm_bank(mm)
                    for c in range(2):
                        m = pe.matmul(bank[:, 0:UQ_N], cqT[:, c, :], small_w[:, c * UQ_N:(c + 1) * UQ_N],
                                      start=c == 0, stop=c == 1)
                    m.then_inc(mm_full, 1)

                if kind == "qm_t":
                    if s == "S":
                        pe.wait_ge(roped, n("roped"))
                    else:
                        pe.wait_ge(mm_free, mm)
                    bank = t_bank(t)
                    for h in range(4):
                        m = pe.transpose(bank[0:96, h * P:(h + 1) * P], qm[:, h * 96:(h + 1) * 96], ident[:])
                    m.then_inc(t_full, 1)

                if kind == "cache_t":
                    pe.wait_ge(cache_in, 16 * (l + 1))
                    bank = t_bank(t)
                    for q, c in enumerate((CA_K, CA_K + P, CA_GK, CA_CKV)):
                        m = pe.transpose(bank[:, q * P:(q + 1) * P], cache[:, c:c + P], ident[:])
                    m.then_inc(t_full, 1)
                    bank = t_bank(t + 1)
                    pe.transpose(bank[0:96, 0:P], cache[:, CA_KR - 64:CA_GK], ident[:]).then_inc(t_full, 1)

                if kind == "kv_mla":
                    pe.wait_ge(t_free, t)
                    ukv = small_w[:, 2 * UQ_N:2 * UQ_N + UKV_N].rearrange("p (h c) -> p h c", h=4)
                    for h in range(4):
                        bank = mm_bank(mm + h)
                        pe.matmul(bank[0:64, 0:K], ukv[:, h, 0:64], ckvT[:, 0:K], start=True, stop=True
                                  ).then_inc(mm_full, 1)
                    for kb in range(KB):
                        bank = mm_bank(mm + 4 + kb)
                        pe.matmul(bank[:, 0:256], ckvT[:, kb * P:(kb + 1) * P], ukv[:, :, 64:128], start=True, stop=True
                                  ).then_inc(mm_full, 1)
                    pe.wait_ge(mm_free, mm + 4 + KB)

                if kind == "heads":
                    first = e * PER_STEP

                    def scores(m, u):
                        bank = mm_bank(u)
                        if m < 8:
                            r = slice(32 * (m % 4), 32 * (m % 4) + 32)
                            q_, k_ = qdT[r, m // 4, cols], kdT[r, m // 4, 0:K]
                        elif m < 12:
                            q_, k_ = qmT[0:96, m - 8, cols], kmT[0:96, m - 8, 0:K]
                        else:
                            v = (m - 12) // 4
                            r = slice(64 * v, 64 * v + 64)
                            q_, k_ = qgT[r, (m - 12) % 4, cols], kgT[r, 0:K]
                        pe.matmul(bank[:, 0:K], q_, k_, start=True, stop=True).then_inc(sc_full, 1)

                    def values(m, kb):
                        own = kb < NB
                        src = proj(B[kb]) if own else cache
                        if m < 8:
                            c = (AV if own else CA_V) + 64 * (m // 2)
                        elif m < 12:
                            return vm[:, kb, 64 * (m - 8):64 * (m - 7)]
                        else:
                            c = (GV if own else CA_GV) + 64 * ((m - 12) // 4)
                        return src[:, c:c + 64]

                    if e in (0, 2, 4):
                        use = n("obank") - 1
                        if use >= 2:
                            pe.wait_ge(o_free, use - 1)
                        obank = ob[use % 2]
                    for i in range(PER_STEP + 1):
                        if i < PER_STEP:
                            scores(first + i, mm + i)
                        if i > 0:
                            m, u = first + i - 1, t + i - 1
                            pe.wait_ge(mm_free, mm + i)
                            bank = t_bank(u)
                            for kb in range(KB):
                                tr = pe.transpose(bank[:, kb * P:(kb + 1) * P],
                                                  E[:, (m) % 2, kb * P:(kb + 1) * P], ident[:])
                            tr.then_inc(t_full, 1)
                            pe.wait_ge(t_free, u + 1)
                            for kb in range(KB):
                                o = pe.matmul(obank[:, (m % 8) * 64:(m % 8) * 64 + 64],
                                              ET[:, m % 2, kb * P:(kb + 1) * P], values(m, kb),
                                              start=kb == 0, stop=kb == KB - 1)
                    if e in (1, 3, 4):
                        o.then_inc(o_full, 1)

                if kind == "r_score":
                    if b == B[0] and e == 0:
                        keys = weights()
                    if e == 0:
                        pe.wait_ge(mm_free, mm)
                        if n("rs") >= 2:
                            pe.wait_ge(idx_ready, n("rs", 0) - 1)
                    bank = mm_bank(mm)
                    for q in range(4):
                        c = 4 * e + q
                        m = pe.matmul(bank[:, q * P:(q + 1) * P], qT[:, c, cols], keys[:, c * P:(c + 1) * P],
                                      start=True, stop=True)
                    m.then_inc(mm_full, 1)

                if kind == "peer":
                    k0, cnt = e
                    if k0 == 0:
                        opened = n("acc")
                        if opened > 1:
                            pe.wait_ge(acc_read, opened - 1)

                    def add_slot(r, start):
                        for half in range(2):
                            cs = slice(half * 512, half * 512 + 512)
                            m = pe.matmul(acc[:, cs], diag[:, r, :], expert[:, r, D + half * 512:D + half * 512 + 512],
                                          start=start, stop=False, skip_group_check=True)
                        m.then_inc(slot_done, 1)

                    for k, bodies, size in slot_runs(k0, cnt, k0 == 0):
                        g = slot + k - k0
                        if bodies > 1:
                            with pe.Fori(0, bodies) as it:
                                for i in range(size):
                                    pe.wait_ge(diag_ready, it * RING + (g + i + 1))
                                    add_slot((g + i) % RING, False)
                        else:
                            for i in range(size):
                                pe.wait_ge(diag_ready, g + i + 1)
                                add_slot((g + i) % RING, k + i == 0)

        @block.scalar
        def _(act):
            n = counter()

            def link(ins):
                ins.then_inc(a_seq, 1)
                act.wait_ge(a_seq, n("a_seq"))

            def mm_copy(dst, src_of, u, rows_=slice(0, P)):
                act.wait_ge(mm_full, n("mm_full"))
                act.activation(dst, src_of(mmb[u % 2]), ACT.Copy).then_inc(mm_free, 1)

            def t_wait(u):
                act.wait_ge(t_full, n("t_full"))
                return trb[u % 2]

            act.wait_ge(const_in, 16 * N_CONST)
            act.activation(cond_e, cond_rows, ACT.Exp, scale=-1.0).then_inc(cond_exp, 1)
            act.wait_ge(lam_dots, 2 * L)
            act.activation(small[:, 8:8 + 2 * L], small[:, 0:2 * L], ACT.Exp).then_inc(lam_exp, 1)

            for (kind, l, s, b, e), mm, t, slot in walk():
                B = BLOCKS.get(s, ())
                NB, KB = len(B), KEYS.get(s, 0)
                K = KB * P
                j = max(b - 1, 0)
                cols = slice(j * P, (j + 1) * P)

                if kind == "cond":
                    bank = t_wait(t)
                    act.activation(csT[:], bank[:, 0:16].rearrange("p (s c) -> p s c", s=2), ACT.Copy).then_inc(t_free, 1)

                if kind == "mod":
                    k = n("mod") - 1
                    if k >= 2:
                        act.wait_ge(mod_stored[(k - 2) % 6], 16 * ((k - 2) // 6 + 1))
                    for c in range(MOD_T):
                        mm_copy(mrow[0:2, k % 2, c * 256:(c + 1) * 256], lambda bk: bk[0:2, 0:256], mm + c)
                    act.wait_ge(mod_row, k + 1)
                    act.dma_start(mod_dram[l, :, b, :], mrow[0:2, k % 2, :]).then_inc(mod_stored[b], 16)

                if kind == "h_t":
                    for half in range(2):
                        bank = t_wait(t + half)
                        act.activation(hT[:, 4 * half:4 * half + 4, cols],
                                       bank[:].rearrange("p (a c) -> p a c", a=4), ACT.Copy).then_inc(t_free, 1)

                if kind == "win":
                    if b == 0:
                        for r in range(6):
                            act.wait_ge(mod_stored[r], 16 * (n("mod", 0) // 6))
                    dst = wide[:, 0:NB * WIN].rearrange("p (j c) -> p j c", j=NB)[:, :, b * IN_C:(b + 1) * IN_C]
                    mm_copy(dst, lambda bk: bk[:, 0:NB * 256].rearrange("p (j c) -> p j c", j=NB)[:, :, 0:IN_C], mm)

                if kind == "prep" and s == "P":
                    act.wait_ge(prep_done, n("prep_out"))
                    p = proj(b)
                    for name, c0, c1 in (("diff_k", AK, AV), ("diff_v", AV, CQ), ("mla_ckv", CKV, KR),
                                         ("mla_krope", KR, GQ), ("gqa_k", GK, GV), ("gqa_v", GV, WIN)):
                        act.dma_start(t_out[name][l], p[:, c0:c1]).then_inc(kv_stored, 16)
                        n("kv_out", 16)
                if kind == "prep" and s == "S":
                    n("prep_out")

                if kind == "prep_t":
                    bank = t_wait(t)
                    act.activation(qdT[:, :, cols], bank[:, 0:256].rearrange("p (a c) -> p a c", a=2), ACT.Copy)
                    act.activation(kdT[:, :, cols], bank[:, 256:512].rearrange("p (a c) -> p a c", a=2), ACT.Copy
                                   ).then_inc(t_free, 1)
                    bank = t_wait(t + 1)
                    act.activation(qgT[:, :, cols], bank[:].rearrange("p (a c) -> p a c", a=4), ACT.Copy).then_inc(t_free, 1)
                    bank = t_wait(t + 2)
                    act.activation(kgT[:, cols], bank[:, 0:P], ACT.Copy)
                    act.activation(ckvT[:, cols], bank[:, P:2 * P], ACT.Copy)
                    for h in range(4):
                        m = act.activation(kmT[64:96, h, cols], bank[64:96, 2 * P:3 * P], ACT.Copy)
                    m.then_inc(t_free, 1)
                    bank = t_wait(t + 3)
                    act.activation(cqT, bank[:, 0:256].rearrange("p (a c) -> p a c", a=2), ACT.Copy).then_inc(t_free, 1)
                    mm_copy(qm, lambda bk: bk[:, 0:UQ_N], mm)

                if kind == "qm_t":
                    bank = t_wait(t)
                    act.activation(qmT[0:96, :, cols], bank[0:96, :].rearrange("p (a c) -> p a c", a=4), ACT.Copy
                                   ).then_inc(t_free, 1)

                if kind == "cache_t":
                    kc = slice(2 * P, 3 * P)
                    bank = t_wait(t)
                    act.activation(kdT[:, :, kc], bank[:, 0:256].rearrange("p (a c) -> p a c", a=2), ACT.Copy)
                    act.activation(kgT[:, kc], bank[:, 256:384], ACT.Copy)
                    act.activation(ckvT[:, kc], bank[:, 384:512], ACT.Copy).then_inc(t_free, 1)
                    bank = t_wait(t + 1)
                    for h in range(4):
                        m = act.activation(kmT[64:96, h, kc], bank[64:96, 0:P], ACT.Copy)
                    m.then_inc(t_free, 1)

                if kind == "kv_mla":
                    for h in range(4):
                        mm_copy(kmT[0:64, h, 0:K], lambda bk: bk[0:64, 0:K], mm + h)
                    for kb in range(KB):
                        mm_copy(vm[:, kb, :], lambda bk: bk[:, 0:256], mm + 4 + kb)

                if kind == "heads":
                    for i in range(PER_STEP + 1):
                        if i < PER_STEP:
                            m = e * PER_STEP + i
                            act.wait_ge(nmax_ready, n("nmax"))
                            act.activation(E[:, m % 2, 0:K], mmb[(mm + i) % 2][:, 0:K], ACT.Exp,
                                           bias=neg_max[:, m:m + 1], scale=SCALE[m],
                                           accum_out=row_sum[:, m:m + 1]).then_inc(mm_free, 1)
                        if i > 0:
                            m = e * PER_STEP + i - 1
                            bank = t_wait(t + i - 1)
                            act.activation(ET[:, m % 2, 0:K], bank[:, 0:K], ACT.Copy).then_inc(t_free, 1)

                if kind == "wout":
                    if b == 0 and s == "P":
                        act.wait_ge(kv_stored, n("kv_out", 0))
                    dst = wide[:, 0:NB * D].rearrange("p (j c) -> p j c", j=NB)[:, :, b * 256:(b + 1) * 256]
                    mm_copy(dst, lambda bk: bk[:, 0:NB * 256].rearrange("p (j c) -> p j c", j=NB), mm)

                if kind == "wq":
                    mm_copy(qT[:, 2 * b:2 * b + 2, 0:NB * P],
                            lambda bk: bk[:].rearrange("p (i c) -> p i c", i=2)[:, :, 0:NB * P], mm)

                if kind == "r_score":
                    mm_copy(rs[:, 4 * e:4 * e + 4, :], lambda bk: bk[:].rearrange("p (i c) -> p i c", i=4), mm)

                if kind == "pick" and e == 1:
                    act.wait_ge(gate_diff, n("gate"))
                    act.activation(gate[:, b, :], gate[:, b, :], ACT.Exp).then_inc(gate_exp, 1)

                if kind == "peer":
                    k0, cnt = e
                    for k, bodies, size in slot_runs(k0, cnt, k0 == 0):
                        g = slot + k - k0
                        if bodies > 1:
                            with act.Fori(0, bodies) as it:
                                for i in range(size):
                                    r = (g + i) % RING
                                    act.wait_ge(dot_ready, it * RING + (g + i + 1))
                                    act.activation(acts[:, r:r + 1], dots[:, r:r + 1], ACT.Gelu_apprx_tanh
                                                   ).then_inc(act_ready, 1)
                        else:
                            for i in range(size):
                                r = (g + i) % RING
                                act.wait_ge(dot_ready, g + i + 1)
                                act.activation(acts[:, r:r + 1], dots[:, r:r + 1], ACT.Gelu_apprx_tanh
                                               ).then_inc(act_ready, 1)
            act.wait_ge(kv_stored, n("kv_out", 0))

        @block.vector
        def _(v):
            n = counter()

            def link(ins):
                ins.then_inc(v_seq, 1)
                v.wait_ge(v_seq, n("v_seq"))

            def inv_sqrt(dst, src, scale):
                w = src.shape[-1]
                val, t = newton[:, 0:w], newton[:, 10:10 + w]
                link(v.tensor_scalar(val, src, scale, EPS, ALU.mult, ALU.add))
                link(v.tensor_scalar(t.bitcast(U32), val.bitcast(U32), 1, None, ALU.logical_shift_right))
                link(v.tensor_scalar(dst.bitcast(U32), t.bitcast(U32), -1.0, float(0x5F3759DF), ALU.mult, ALU.add))
                for _ in range(3):
                    link(v.tensor_tensor(t, dst, dst, ALU.mult))
                    link(v.scalar_tensor_tensor(out=t, in0=t, scalar=-0.5, in1=val, op0=ALU.mult, op1=ALU.mult))
                    link(v.scalar_tensor_tensor(out=dst, in0=t, scalar=1.5, in1=dst, op0=ALU.add, op1=ALU.mult))

            def normed(dst, src):
                for c in range(2):
                    link(v.bn_stats(small[:, 16 + 6 * c:22 + 6 * c], src[:, c * 512:(c + 1) * 512]))
                link(v.bn_aggr(small[:, 28:30], small[:, 16:28]))
                inv_sqrt(small[:, 30:31], small[:, 29:30], 1.0)
                link(v.tensor_scalar(dst, src, small[:, 28:29], small[:, 30:31], ALU.subtract, ALU.mult))

            def rms(p, c0, c1, g0, l):
                link(v.tensor_tensor_reduce(t1[:, 0:c1 - c0], p[:, c0:c1], p[:, c0:c1], 1.0, 0.0,
                                            ALU.mult, ALU.add, small[:, 32:33]))
                inv_sqrt(small[:, 33:34], small[:, 32:33], 1.0 / (c1 - c0))
                link(v.scalar_tensor_tensor(out=p[:, c0:c1], in0=p[:, c0:c1], scalar=small[:, 33:34],
                                            in1=gain[:, l, g0:g0 + c1 - c0], op0=ALU.mult, op1=ALU.mult))

            def head_rms(p, heads, gains):
                w = heads * 64
                a = t1[:, 0:w].rearrange("p (h d) -> p h d", d=64)
                p3 = p.rearrange("p (h d) -> p h d", d=64)
                link(v.tensor_tensor(t1[:, 0:w], p, p, ALU.mult))
                link(v.tensor_reduce(small[:, 34:34 + heads], a, X, ALU.add))
                inv_sqrt(small[:, 34:34 + heads], small[:, 34:34 + heads], 1.0 / 64)
                link(v.tensor_tensor(p3, p3, small[:, 34:34 + heads].unsqueeze(2).to_broadcast([P, heads, 64]), ALU.mult))
                for h0, h1, g in gains:
                    link(v.tensor_tensor(p3[:, h0:h1], p3[:, h0:h1], g.unsqueeze(1).to_broadcast([P, h1 - h0, 64]),
                                         ALU.mult))

            def rotate(p3, groups, half, table):
                w = 2 * half
                cos, sin = table[:, 0:w], table[:, w:2 * w]
                a = t1[:, 0:groups * w].rearrange("p (g w) -> p g w", w=w)
                c = t2[:, 0:groups * w].rearrange("p (g w) -> p g w", w=w)
                link(v.tensor_tensor(a, p3, cos.unsqueeze(1).to_broadcast([P, groups, w]), ALU.mult))
                link(v.tensor_tensor(c[:, :, 0:half], p3[:, :, half:w],
                                     sin[:, 0:half].unsqueeze(1).to_broadcast([P, groups, half]), ALU.mult))
                link(v.tensor_tensor(c[:, :, half:w], p3[:, :, 0:half],
                                     sin[:, half:w].unsqueeze(1).to_broadcast([P, groups, half]), ALU.mult))
                link(v.tensor_tensor(p3, a, c, ALU.add))

            def group_rows(first):
                if first:
                    g = n("group") - 1
                    dmas = 2 if GROUPS[g][2] in ("g1", "g2") else 1
                    v.wait_ge(rows_in[g % 2], n(f"rows{g % 2}", 16 * dmas))
                return rows[:, (n("group", 0) - 1) % 2]

            v.wait_ge(const_in, 16 * N_CONST)
            for l in range(L):
                for i in range(2):
                    v.tensor_tensor_reduce(t1[:, 64 * l + 32 * i:64 * l + 32 * i + 32], dlam[:, l, 64 * i:64 * i + 32],
                                           dlam[:, l, 64 * i + 32:64 * i + 64], 1.0, 0.0,
                                           ALU.mult, ALU.add, small[:, 2 * l + i:2 * l + i + 1]).then_inc(lam_dots, 1)
                link(v.tensor_scalar(gain[:, l, G_SUB:G_KV], gain[:, l, G_SUB:G_KV], 1.0 - lambda_init(l), None, ALU.mult))
            v.wait_ge(cond_exp, 1)
            link(v.tensor_scalar(cond_e, cond_e, 1.0, None, ALU.add))
            link(v.reciprocal(cond_e, cond_e))
            v.tensor_tensor(cond_rows, cond_rows, cond_e, ALU.mult).then_inc(cond_silu, 1)
            v.wait_ge(lam_exp, 1)
            for l in range(L):
                link(v.tensor_scalar(neglam[:, l:l + 1], small[:, 9 + 2 * l:10 + 2 * l], small[:, 8 + 2 * l:9 + 2 * l],
                                     -lambda_init(l), ALU.subtract, ALU.add))

            for (kind, l, s, b, e), mm, t, slot in walk():
                B = BLOCKS.get(s, ())
                NB, KB = len(B), KEYS.get(s, 0)
                K = KB * P
                p = proj(b) if kind == "prep" else None

                if kind == "mod":
                    k = n("mod") - 1
                    v.wait_ge(bias_in[k % 2], 16 * (k // 2 + 1))
                    v.wait_ge(mm_free, mm + MOD_T)
                    v.scalar_tensor_tensor(out=mrow[0:2, k % 2, :], in0=mrow[0:2, k % 2, :],
                                           scalar=1.0 if b in (1, 4) else 0.0, in1=brow[0:2, k % 2, :],
                                           op0=ALU.add, op1=ALU.add).then_inc(mod_row, 1)

                if kind == "ln1":
                    v.wait_ge(t_free, t)
                    normed(tok[:], x[:, b, :])
                    g = group_rows(b == B[0])
                    link(v.tensor_tensor(tok[:], tok[:], g[:, 1, :], ALU.mult))
                    ins = v.tensor_tensor(tok[:], tok[:], g[:, 0, :], ALU.add)
                    ins.then_inc(tok_ready, 1)
                    v.wait_ge(tok_ready, n("tok"))
                    if b == B[-1]:
                        v.sem_inc(rows_used, 1)

                if kind == "prep":
                    v.wait_ge(mm_free, mm)
                    rms(p, CQ, CKV, G_CQ, l)
                    rms(p, CKV, KR, G_KV, l)
                    head_rms(p[:, GQ:GV], 10, ((0, 8, gain[:, l, G_Q:G_K]), (8, 10, gain[:, l, G_K:G_SUB])))
                    if s == "S":
                        tb = rope[:, b - 1, :]
                        rotate(p[:, AQ:AV].rearrange("p (g w) -> p g w", w=32), 16, 16, tb[:, 0:64])
                        rotate(p[:, KR:GQ].rearrange("p (g w) -> p g w", w=32), 1, 16, tb[:, 0:64])
                        rotate(p[:, GQ:GV].rearrange("p (g w) -> p g w", w=64), 10, 32, tb[:, 64:192])
                    v.sem_inc(prep_done, 1)

                if kind == "q_rope" and s == "S":
                    v.wait_ge(mm_free, mm)
                    rotate(qm.rearrange("p (h d) -> p h d", d=96)[:, :, 64:96], 4, 16, rope[:, b - 1, 0:64])
                    v.sem_inc(roped, 1)

                if kind == "heads":
                    for i in range(PER_STEP):
                        m = e * PER_STEP + i
                        v.wait_ge(sc_full, n("sc"))
                        link(v.reduce_max(neg_max[:, m:m + 1], mmb[(mm + i) % 2][:, 0:K], X))
                        v.tensor_scalar(neg_max[:, m:m + 1], neg_max[:, m:m + 1], -SCALE[m], None, ALU.mult
                                        ).then_inc(nmax_ready, 1)
                    if e in (1, 3, 4):
                        use = n("obank") - 1
                        m0 = 8 * {1: 0, 3: 1, 4: 2}[e]
                        cnt = min(8, MATS - m0)
                        v.wait_ge(o_full, use + 1)
                        link(v.reciprocal(small[:, 46:46 + cnt], row_sum[:, m0:m0 + cnt]))
                        dst = od if m0 == 0 else tok[:, 64 * (m0 - 4):64 * (m0 - 4 + cnt)]
                        v.tensor_tensor(dst.rearrange("p (h d) -> p h d", d=64),
                                        ob[use % 2][:, 0:64 * cnt].rearrange("p (h d) -> p h d", d=64),
                                        small[:, 46:46 + cnt].unsqueeze(2).to_broadcast([P, cnt, 64]),
                                        ALU.mult).then_inc(o_free, 1)
                        v.wait_ge(o_free, use + 1)

                if kind == "mix":
                    pair = od.rearrange("p (h c d) -> p h c d", c=2, d=64)
                    dst = tok[:, 0:256]
                    link(v.scalar_tensor_tensor(out=dst.rearrange("p (h d) -> p h d", d=64), in0=pair[:, :, 1],
                                                scalar=neglam[:, l:l + 1], in1=pair[:, :, 0],
                                                op0=ALU.mult, op1=ALU.add))
                    head_rms(dst, 4, ((0, 4, gain[:, l, G_SUB:G_KV]),))
                    v.sem_inc(tok_ready, 1)
                    n("tok")

                if kind == "ln_x":
                    v.wait_ge(mm_free, mm)
                    g = group_rows(b == B[0])
                    y = ymix(b)
                    link(v.tensor_tensor(y, y, g[:, 0, :], ALU.mult))
                    link(v.scalar_tensor_tensor(out=y, in0=x[:, b, :], scalar=ALPHA, in1=y, op0=ALU.mult, op1=ALU.add))
                    normed(y, y)
                    link(v.tensor_tensor(y, y, g[:, 1, :], ALU.mult))
                    link(v.tensor_tensor(x[:, b, :], y, g[:, 2, :], ALU.add))
                    if b == B[-1]:
                        v.sem_inc(rows_used, 1)

                if kind == "ln_h":
                    g = group_rows(b == B[0])
                    normed(h2[:, b, :], x[:, b, :])
                    link(v.tensor_tensor(h2[:, b, :], h2[:, b, :], g[:, 1, :], ALU.mult))
                    link(v.tensor_tensor(h2[:, b, :], h2[:, b, :], g[:, 0, :], ALU.add))
                    v.sem_inc(h2_ready, 1)
                    if b == B[-1]:
                        v.sem_inc(rows_used, 1)

                if kind == "topk":
                    if e == 0:
                        v.wait_ge(mm_free, mm)
                    for c in (2 * e, 2 * e + 1):
                        link(v.max(v16[:, c, 0:8], rs[:, c, :]))
                        link(v.max_index(i16[:, c, 0:8], v16[:, c, 0:8], rs[:, c, :]))
                        link(v.match_replace(rep, v16[:, c, 0:8], rs[:, c, :], -3e38))
                        link(v.max(v16[:, c, 8:16], rep))
                        link(v.max_index(i16[:, c, 8:16], v16[:, c, 8:16], rep))
                    flat = cand.rearrange("p a c -> p (a c)")
                    link(v.tensor_tensor(cand, v16[:, 2 * e, :].unsqueeze(2).to_broadcast([P, 16, 16]),
                                         v16[:, 2 * e + 1, :].unsqueeze(1).to_broadcast([P, 16, 16]), ALU.add))
                    link(v.max(best[:, e, 0:8], flat))
                    link(v.max_index(bi[:, e, 0:8], best[:, e, 0:8], flat))
                    link(v.match_replace(cand2, best[:, e, 0:8], flat, -3e38))
                    link(v.max(best[:, e, 8:16], cand2))
                    link(v.max_index(bi[:, e, 8:16], best[:, e, 8:16], cand2))

                if kind == "pick":
                    bflat = bi[:].rearrange("p h k -> p (h k)")
                    if e == 0:
                        link(v.tensor_copy(i16f, i16[:].rearrange("p (h c) k -> p h c k", c=2)))
                        link(v.tensor_scalar(bit[:], bflat, 4, None, ALU.logical_shift_right))
                    else:
                        link(v.tensor_scalar(bit[:], bflat, 15, None, ALU.bitwise_and))
                    link(v.tensor_copy(bf, bit[:]))
                    link(v.tensor_tensor(eq.rearrange("p h k i -> p (h k) i"),
                                         iota[:].unsqueeze(1).to_broadcast([P, SLOTS, 16]),
                                         bf.unsqueeze(2).to_broadcast([P, SLOTS, 16]), ALU.is_equal))
                    link(v.tensor_tensor(eq, eq, i16f[:, :, e, :].unsqueeze(2).to_broadcast([P, R_HEADS, TOPK, 16]),
                                         ALU.mult))
                    link(v.tensor_reduce(e1 if e == 0 else e2, eq.rearrange("p h k i -> p (h k) i"), X, ALU.add))
                    if e == 1:
                        g3 = gate[:, b, :].rearrange("p (h k) -> p h k", h=R_HEADS)
                        v.tensor_tensor(g3, best, best[:, :, 0:1].to_broadcast([P, R_HEADS, TOPK]),
                                        ALU.subtract).then_inc(gate_diff, 1)
                        link(v.tensor_scalar(e1, e1, 128.0, float(l * N_EXP), ALU.mult, ALU.add))
                        link(v.tensor_tensor(eidx[:, b, :], e1, e2, ALU.add))
                        v.wait_ge(gate_exp, n("gate"))
                        link(v.tensor_reduce(small[:, 54:62], g3, X, ALU.add))
                        link(v.reciprocal(small[:, 54:62], small[:, 54:62]))
                        link(v.tensor_tensor(g3, g3, small[:, 54:62].unsqueeze(2).to_broadcast([P, R_HEADS, TOPK]),
                                             ALU.mult))
                        v.sem_inc(idx_ready, 1)

                if kind == "peer":
                    k0, cnt = e

                    def dot(r):
                        v.tensor_tensor_reduce(expert[:, r, 0:D], expert[:, r, 0:D], h2[:, b, :], 1.0, 0.0,
                                               ALU.mult, ALU.add, dots[:, r:r + 1]).then_inc(dot_ready, 1)

                    def weigh(r, col):
                        v.tensor_scalar(diag[:, r, :], ident[:], acts[:, r:r + 1], col, ALU.mult, ALU.mult
                                        ).then_inc(diag_ready, 1)

                    for k, bodies, size in slot_runs(k0, cnt, k0 == 0):
                        g = slot + k - k0
                        if bodies > 1:
                            with v.Fori(0, bodies) as it:
                                for i in range(size + 1):
                                    if i < size:
                                        q = g + i
                                        v.wait_ge(landed[q % RING], it * 16 + 16 * (q // RING + 1))
                                        dot(q % RING)
                                    if i > 0:
                                        v.wait_ge(act_ready, it * RING + (g + i))
                                        weigh((g + i - 1) % RING, gate[:, b, bass.ds(it * RING + (k + i - 1), 1)])
                        else:
                            for i in range(size + 1):
                                if i < size:
                                    q = g + i
                                    v.wait_ge(landed[q % RING], 16 * (q // RING + 1))
                                    dot(q % RING)
                                if i > 0:
                                    v.wait_ge(act_ready, g + i)
                                    weigh((g + i - 1) % RING, gate[:, b, k + i - 1:k + i])

                if kind == "fin":
                    g = group_rows(True)
                    z = tmp[:, 0:D]
                    v.wait_ge(slot_done, slot)
                    v.tensor_tensor(z, acc[:], g[:, 0, :], ALU.mult).then_inc(acc_read, 1)
                    v.wait_ge(acc_read, n("acc"))
                    link(v.scalar_tensor_tensor(out=z, in0=x[:, b, :], scalar=ALPHA, in1=z, op0=ALU.mult, op1=ALU.add))
                    normed(z, z)
                    link(v.tensor_tensor(z, z, g[:, 1, :], ALU.mult))
                    link(v.tensor_tensor(x[:, b, :], z, g[:, 2, :], ALU.add))
                    v.sem_inc(rows_used, 1)
                    if l == L - 1:
                        v.sem_inc(y_ready, 1)


N_CONST = 9

_OUTS = (("y_prompt", (P, D)), ("y_sample", (2 * P, D)), ("diff_k", (L, P, 256)), ("diff_v", (L, P, 256)),
         ("mla_ckv", (L, P, 128)), ("mla_krope", (L, P, 32)), ("gqa_k", (L, P, 128)), ("gqa_v", (L, P, 128)))


def _tiled(w, width):
    import numpy as np
    layers, rows, cols = w.shape
    v = w.reshape(layers, rows // P, P, cols // width, width)
    return np.ascontiguousarray(v.transpose(0, 3, 2, 1, 4)).reshape(layers, cols // width, P, rows // P * width)


def _rotary():
    import numpy as np
    f = np.float32
    t = np.arange(2 * P)
    out = []
    for dim in (32, 64):
        n = dim // 4
        inv = f(10000.0) ** (-np.arange(n, dtype=f) / f(n))
        ang = np.concatenate([(t // GRID_W).astype(f)[:, None] * inv, (t % GRID_W).astype(f)[:, None] * inv], axis=-1)
        c, s = np.cos(ang), np.sin(ang)
        out += [c, c, -s, s]
    return np.ascontiguousarray(np.concatenate(out, axis=-1).reshape(2, P, 192).transpose(1, 0, 2), dtype=f)


def kernel(x_prompt, x_sample, c, cache_diff_k, cache_diff_v, cache_mla_ckv, cache_mla_krope,
           cache_gqa_k, cache_gqa_v, c_ctx, w_mod, b_mod, w_in, diff_lambda, diff_subln_g,
           mla_q_norm_g, mla_kv_norm_g, mla_w_uq, mla_w_ukv, gqa_q_norm_g, gqa_k_norm_g, w_out,
           ln1_g, ln1_b, ln2_g, ln2_b, peer_wq, peer_keys, peer_u, peer_v):
    import numpy as np
    import concourse.bacc as bacc
    from concourse.bass_utils import run_bass_kernel_spmd

    A = np.asarray
    cat = np.concatenate
    cache = cat([A(a).reshape(L, PAST, -1) for a in (cache_diff_k, cache_diff_v, cache_mla_ckv, cache_mla_krope,
                                                     cache_gqa_k, cache_gqa_v)], axis=-1)
    uq = A(mla_w_uq).reshape(L, 2, P, UQ_N).transpose(0, 2, 1, 3).reshape(L, P, 2 * UQ_N)
    w_in = cat([A(w_in)[:, :, :GQ],
                A(w_in)[:, :, GQ:GK].reshape(L, D, 2, 4, 64).transpose(0, 1, 3, 2, 4).reshape(L, D, 512),
                A(w_in)[:, :, GK:]], axis=-1)
    arrays = {
        "ident": np.eye(P, dtype=np.float32),
        "iota": np.tile(np.arange(TOPK, dtype=np.float32), (P, 1)),
        "rope": _rotary(),
        "cond": cat([A(c_ctx).reshape(KT, P), A(c).reshape(KT, P)]),
        "gain": cat([A(gqa_q_norm_g), A(gqa_k_norm_g), A(diff_subln_g), A(mla_kv_norm_g), A(mla_q_norm_g)], axis=-1),
        "dlam": A(diff_lambda).reshape(L, P),
        "x_prompt": A(x_prompt).reshape(P, D),
        "x_sample": A(x_sample).reshape(2 * P, D),
        "cache": cache,
        "w_mod": _tiled(A(w_mod), 256),
        "b_mod": A(b_mod).reshape(L, 6, D),
        "w_win": _tiled(A(w_in), IN_C),
        "w_small": cat([uq, A(mla_w_ukv)], axis=-1).reshape(L, 1, P, 2 * UQ_N + UKV_N),
        "w_wout": _tiled(A(w_out), 256),
        "ln": np.stack([A(ln1_g), A(ln1_b), A(ln2_g), A(ln2_b)], axis=1).reshape(L, 2, 2, D),
        "w_wq": _tiled(A(peer_wq), 256),
        "w_keys": A(peer_keys).reshape(L, 16, P, P).transpose(0, 3, 1, 2).reshape(L, 1, P, 16 * P),
        "experts": cat([A(peer_u), A(peer_v)], axis=-1).reshape(L * N_EXP, 2 * D),
    }
    arrays = {k: np.ascontiguousarray(v) for k, v in arrays.items()}
    nc = bacc.Bacc("TRN2", target_bir_lowering=False, num_devices=1)
    t_in = {k: nc.dram_tensor(f"in_{k}", v.shape, F32, kind="ExternalInput").ap() for k, v in arrays.items()}
    t_out = {k: nc.dram_tensor(f"out_{k}", shape, F32, kind="ExternalOutput").ap() for k, shape in _OUTS}
    trunk_program(nc, t_in, t_out)
    r = run_bass_kernel_spmd(nc, [{f"in_{k}": v for k, v in arrays.items()}], core_ids=[0]).results[0]
    o = {k: np.asarray(r[f"out_{k}"]) for k, _ in _OUTS}
    return (o["y_prompt"].reshape(1, P, D), o["y_sample"].reshape(1, 2 * P, D),
            o["diff_k"].reshape(1, L, P, 4, 2, 32), o["diff_v"].reshape(1, L, P, 4, 64),
            o["mla_ckv"].reshape(1, L, P, 128), o["mla_krope"].reshape(1, L, P, 32),
            o["gqa_k"].reshape(1, L, P, 2, 64), o["gqa_v"].reshape(1, L, P, 2, 64))
```

```python
import math
from contextlib import ExitStack

import concourse.bass as bass
from concourse import mybir

F32 = mybir.dt.float32
I32 = mybir.dt.int32
U32 = mybir.dt.uint32
ALU = mybir.AluOpType
ACT = mybir.ActivationFunctionType
X = mybir.AxisListType.X

P = 128
D = 1024
KT = D // P
L = 2
PAST = 128
GRID_W = 64
EPS = 1e-6
ALPHA = (2 * L) ** 0.25
N_EXP = 128 * 128
TOPK = 16
R_HEADS = 8
SLOTS = R_HEADS * TOPK
AQ, AK, AV, CQ, CKV, KR, GQ, GK, GV, WIN = 0, 256, 512, 768, 1024, 1152, 1184, 1696, 1824, 1952
CA_K, CA_V, CA_CKV, CA_KR, CA_GK, CA_GV, CA_N = 0, 256, 512, 640, 672, 800, 928
G_Q, G_K, G_SUB, G_KV, G_CQ, G_N = 0, 64, 128, 192, 320, 576
WT = 2048 + 256
IN_T = 8
IN_C = WIN // IN_T
OUT_T = 4
WQ_T = 8
MOD_T = 4
UQ_N = 384
UKV_N = 512
MATS = 20
PER_STEP = 4
SCALE = [32 ** -0.5] * 8 + [96 ** -0.5] * 4 + [64 ** -0.5] * 8
RING = 6
GRAIN = 6
WRING = 3
RROWS = 4

BLOCKS = {"P": (0,), "S": (1, 2)}
KEYS = {"P": 1, "S": 3}


def lambda_init(l):
    return 0.8 - 0.6 * math.exp(-0.3 * l)


COST = {"mod": 4, "ln1": 6, "win": 4, "prep": 12, "k_t": 5, "q_t": 5, "q_rope": 3, "qm_t": 2, "cache_t": 3,
        "kv_mla": 5, "heads": 9, "mix": 5, "h_t": 3, "wout": 4, "ln_x": 9, "ln_h": 7, "route": 6, "pick": 9}


def common_steps(l, s):
    out = []
    for b in BLOCKS[s]:
        out += [("ln1", l, s, b, 0), ("h_t", l, s, b, 0)]
    out += [("win", l, s, n, 0) for n in range(IN_T)]
    for b in BLOCKS[s]:
        out += [("prep", l, s, b, 0), ("k_t", l, s, b, 0)]
    if s == "S":
        out += [("cache_t", l, s, 0, 0)]
    return out + [("kv_mla", l, s, 0, 0)]


def block_steps(l, s, b):
    out = [("q_t", l, s, b, 0), ("q_rope", l, s, b, 0), ("qm_t", l, s, b, 0)]
    out += [("heads", l, s, b, i) for i in range(MATS // PER_STEP)]
    out += [("mix", l, s, b, 0), ("h_t", l, s, b, 1)]
    out += [("wout", l, s, b, n) for n in range(OUT_T)]
    out += [("ln_x", l, s, b, 0), ("ln_h", l, s, b, 0), ("h_t", l, s, b, 2)]
    out += [("route", l, s, b, n) for n in range(WQ_T + 1)]
    return out + [("pick", l, s, b, c) for c in range(2)]


def mod_steps(l, rows_=range(6)):
    return [("mod", l, "", row, c) for row in rows_ for c in range(MOD_T)]


def fill(steps, fillers, after):
    out, todo = [], list(fillers)
    for x in steps:
        out.append(x)
        n = after.get(x[0], 0)
        out += todo[:n]
        todo = todo[n:]
    return out + todo


def weave(l, b, steps):
    total = sum(COST[x[0]] for x in steps) or 1
    out, done, cost = [], 0, 0
    for x in steps:
        out.append(x)
        cost += COST[x[0]]
        at = (SLOTS * cost // total) // GRAIN * GRAIN
        if at > done:
            out.append(("peer", l, "", b, (done, at - done)))
            done = at
    if done < SLOTS:
        out.append(("peer", l, "", b, (done, SLOTS - done)))
    return out + [("fin", l, "", b, 0)]


def plan():
    steps = [("cond", 0, "", 0, 0)] + mod_steps(0, (0, 1))
    steps += fill(common_steps(0, "P") + block_steps(0, "P", 0), mod_steps(0, (2, 3, 4, 5)),
                  {"ln1": 2, "prep": 3, "heads": 1, "mix": 2, "ln_x": 2, "ln_h": 2})
    steps += weave(0, 0, common_steps(0, "S") + block_steps(0, "S", 1))
    steps += weave(0, 1, block_steps(0, "S", 2) + mod_steps(1, (0, 1)))
    steps += weave(0, 2, fill(common_steps(1, "P") + block_steps(1, "P", 0), mod_steps(1, (2, 3, 4, 5)),
                              {"ln1": 2, "prep": 3, "heads": 1, "mix": 2, "ln_x": 2, "ln_h": 2}))
    steps += weave(1, 0, common_steps(1, "S") + block_steps(1, "S", 1))
    steps += weave(1, 1, block_steps(1, "S", 2))
    steps += weave(1, 2, [])
    return steps


STEPS = plan()


def banks_used(x):
    kind, l, s, i, e = x
    if kind == "heads":
        return PER_STEP, PER_STEP - (e == 0) + (e == MATS // PER_STEP - 1)
    if kind == "route":
        return (e < WQ_T) + (e > 0), 0
    return {"cond": (0, 1), "mod": (1, 0), "h_t": (0, 2), "win": (1, 0), "k_t": (0, 2), "q_t": (1, 2), "qm_t": (0, 1),
            "cache_t": (0, 2), "kv_mla": (4 + KEYS.get(s, 0), 0), "wout": (1, 0)}.get(kind, (0, 0))


def walk():
    mm = t = slot = 0
    for x in STEPS:
        yield x, mm, t, slot
        a, b = banks_used(x)
        mm, t = mm + a, t + b
        if x[0] == "peer":
            slot += x[4][1]


def load_plan():
    at = list(enumerate(STEPS))
    tiles, rows_, biases = [], [], []
    stored = {}
    for i, (kind, l, s, b, e) in at:
        if kind == "mod":
            tiles.append([("mod", l, MOD_T * b + e), i, i])
            if e == 0:
                biases.append([("bias", l, b), i, i])
            if e == MOD_T - 1:
                biases[-1][2] = i
                stored[l, b] = i
        if kind == "win":
            tiles.append([("win", l, b), i, i])
        if kind == "kv_mla":
            tiles.append([("ukv", l, 0), i, i])
        if kind == "q_t":
            tiles.append([("uq", l, 0), i, i])
        if kind == "wout":
            tiles.append([("wout", l, e), i, i])
        if kind == "route" and e < WQ_T:
            tiles.append([("wq", l, e), i, i + 1])
        if kind == "route" and e > 0:
            tiles[-1 - (e < WQ_T)][2] = i
        st = {"P": 0, "S": 1}.get(s, int(b > 0))
        want = {"ln1": (1, 0), "ln_x": (2, "1g", "1b"), "ln_h": (4, 3), "fin": (5, "2g", "2b")}.get(kind, ())
        if kind == "ln1" and b == 2:
            for r in (-2, -1):
                rows_[r][2] = i
            want = ()
        rows_ += [[("row", l, st, r), i, i] for r in want]
    out = []
    for ring, depth, items in (("tile", WRING, tiles), ("row", RROWS, rows_), ("bias", 1, biases)):
        for n, (what, first, last) in enumerate(items):
            issue = items[n - depth][2] + 1 if n >= depth else 0
            if ring == "row" and not isinstance(what[3], str):
                issue = max(issue, stored[what[1], what[3]] + 1)
            if ring == "bias" and what[1] > 0 and what[2] == 0:
                issue = max(issue, max(i for i, x in at if x[0] == "route" and x[1] == what[1] - 1 and x[3] == 2) + 1)
            assert issue <= first, (what, issue, first)
            out.append((issue, first, ring, n, what))
    for l in range(L):
        ends = [i for i, x in at if x[0] == "heads" and x[1] == l - 1 and x[3] == 2]
        out.append((max(ends) + 2 if ends else 0, max(ends or [0]) + 3, "cache", l, ("cache", l)))
    return sorted(out, key=lambda x: (x[0], x[1])), tiles, rows_


def slot_runs(k, n, peel):
    out = []
    if peel:
        out.append((0, 1, 1))
        k, n = k + 1, n - 1
    if n // RING >= 2:
        out.append((k, n // RING, RING))
        k, n = k + n // RING * RING, n % RING
    while n:
        m = min(n, RING)
        out.append((k, 1, m))
        k, n = k + m, n - m
    return out


def trunk_program(nc, t_in, t_out):
    with ExitStack() as ctx:
        def sb(name, shape, dt=F32):
            return ctx.enter_context(nc.sbuf_tensor(name, shape, dt))

        def ps(name, shape):
            return ctx.enter_context(nc.psum_tensor(name, shape, F32))

        def sem(name):
            return ctx.enter_context(nc.semaphore(name))

        expert = sb("expert", [P, RING, 2 * D])
        wt = sb("wt", [P, WRING, WT])
        rows = sb("rows", [P, RROWS, D])
        x = sb("x", [P, 3, D])
        h2 = sb("h2", [P, 2, D])
        hT = sb("hT", [P, KT, 2 * P])
        wide = sb("wide", [P, 4096])
        tok = sb("tok", [P, D])
        tmp = sb("tmp", [P, 1280])
        area = sb("area", [P, 7808])
        router = sb("router", [P, 3712])
        cache = sb("cache", [P, CA_N])
        ident = sb("ident", [P, P])
        iota = sb("iota", [P, TOPK])
        rope = sb("rope", [P, 2, 192])
        gain = sb("gain", [P, L, G_N])
        neglam = sb("neglam", [P, L])
        small = sb("small", [P, 64])
        newton = sb("newton", [P, 20])
        neg_max = sb("neg_max", [P, MATS])
        row_sum = sb("row_sum", [P, MATS])
        csT = sb("csT", [P, 2, KT])
        i16 = sb("i16", [P, 16, TOPK], U32)
        bi = sb("bi", [P, R_HEADS, TOPK], U32)
        bit = sb("bit", [P, SLOTS], U32)
        eidx = sb("eidx", [P, 2, SLOTS], I32)
        gate = sb("gate", [P, 2, SLOTS])
        dots = sb("dots", [P, RING])
        acts = sb("acts", [P, RING])
        diag = sb("diag", [P, RING, P])
        mod_dram = nc.dram_tensor("mod_scratch", (L, 2, 6, D), F32, kind="Internal").ap()

        acc = ps("acc", [P, D])
        mmb = [ps(f"mmb{i}", [P, 512]) for i in range(2)]
        trb = [ps(f"trb{i}", [P, 512]) for i in range(2)]
        ob = [ps(f"ob{i}", [P, 512]) for i in range(2)]

        def cut(t, at, shape):
            n = int(math.prod(shape))
            v = t[:, at:at + n]
            if len(shape) == 2:
                v = v.rearrange("p (a b) -> p a b", b=shape[1])
            if len(shape) == 3:
                v = v.rearrange("p (a b c) -> p a b c", b=shape[1], c=shape[2])
            return v

        def proj(b):
            j = max(b - 1, 0)
            return wide[:, j * WIN:(j + 1) * WIN]

        def part(l, b):
            return (3 * l + b) % 2

        mrow = wide[:, 2 * D:3 * D]
        brow = wide[:, 3 * D:4 * D]
        at = 0
        views = {}
        for name, shape in (("qdT", (2, P)), ("qgT", (4, P)), ("qmT", (4, P)), ("kdT", (2, 384)),
                            ("kgT", (384,)), ("kmT", (4, 384)), ("ckvT", (384,)), ("vm", (3, 256)),
                            ("qm", (UQ_N,)), ("cqT", (2, P)), ("E", (2, 384)), ("ET", (2, 384)), ("od", (512,))):
            views[name] = cut(area, at, shape)
            at += int(math.prod(shape))
        assert at == 7808, at
        qdT, qgT, qmT, kdT, kgT, kmT, ckvT, vm, qm, cqT, E, ET, od = views.values()
        at = 0
        views = {}
        for name, shape in (("qT", (2, 2, P)), ("rs", (2, 2, P)), ("rep", (2, P)), ("cand", (16, 16)), ("cand2", (256,)),
                            ("eq", (4, TOPK, 16)), ("v16", (16, TOPK)), ("i16f", (R_HEADS, 2, TOPK)),
                            ("best", (R_HEADS, TOPK)), ("bf", (SLOTS,)), ("e1", (SLOTS,))):
            views[name] = cut(router, at, shape)
            at += int(math.prod(shape))
        assert at <= 3712, at
        qT, rs, rep, cand, cand2, eq, v16, i16f, best, bf, e1 = views.values()
        e2 = cand2[:, 0:SLOTS]
        dlam = cut(area, 0, (L, P))
        cond_rows = area[0:2 * KT, L * P:L * P + P]
        cond_e = area[0:2 * KT, L * P + P:L * P + 2 * P]
        t1, t2 = tmp[:, 0:640], tmp[:, 640:1280]

        const_in = sem("const_in")
        cache_in = sem("cache_in")
        w_in_slot = [sem(f"w_in_slot{i}") for i in range(WRING)]
        rows_in = [sem(f"rows_in{i}") for i in range(RROWS)]
        rows_used = sem("rows_used")
        bias_in = sem("bias_in")
        mod_row = sem("mod_row")
        mod_stored = [sem(f"mod_stored{i}") for i in range(6)]
        mm_full = sem("mm_full")
        mm_free = sem("mm_free")
        t_full = sem("t_full")
        t_free = sem("t_free")
        sc_full = sem("sc_full")
        nmax_ready = sem("nmax_ready")
        o_full = sem("o_full")
        o_free = sem("o_free")
        lam_dots = sem("lam_dots")
        lam_exp = sem("lam_exp")
        cond_exp = sem("cond_exp")
        cond_silu = sem("cond_silu")
        tok_ready = sem("tok_ready")
        h2_ready = sem("h2_ready")
        prep_done = sem("prep_done")
        roped = sem("roped")
        kv_stored = sem("kv_stored")
        gate_diff = sem("gate_diff")
        gate_exp = sem("gate_exp")
        topk_done = sem("topk_done")
        idx_ready = sem("idx_ready")
        landed = [sem(f"landed{i}") for i in range(RING)]
        dot_ready = sem("dot_ready")
        act_ready = sem("act_ready")
        diag_ready = sem("diag_ready")
        slot_done = sem("slot_done")
        acc_read = sem("acc_read")
        y_ready = sem("y_ready")
        y_stored = sem("y_stored")
        v_seq = sem("v_seq")
        a_seq = sem("a_seq")

        def counter():
            seen = {}

            def count(name, n=1):
                seen[name] = seen.get(name, 0) + n
                return seen[name]
            return count

        loads, tile_uses, row_uses = load_plan()
        mm_after = [mm + banks_used(x)[0] for x, mm, _, _ in walk()]

        block = ctx.enter_context(nc.Block())

        @block.sync
        def _(sp):
            for dst, src in ((ident[:], t_in["ident"]), (cond_rows, t_in["cond"]), (iota[:], t_in["iota"]),
                             (rope[:], t_in["rope"]), (gain[:], t_in["gain"].partition_broadcast(P)),
                             (dlam, t_in["dlam"].partition_broadcast(P)),
                             (x[:, 0, :], t_in["x_prompt"]), (x[:, 1, :], t_in["x_sample"][0:P, :]),
                             (x[:, 2, :], t_in["x_sample"][P:2 * P, :])):
                sp.dma_start(dst, src).then_inc(const_in, 16)
            for _, _, ring, n, what in loads:
                if ring == "tile":
                    if n >= WRING:
                        sp.wait_ge(mm_free, mm_after[tile_uses[n - WRING][2]])
                    src = t_in["w_" + what[0]][what[1], what[2]]
                    sp.dma_start(wt[:, n % WRING, 0:src.shape[-1]], src).then_inc(w_in_slot[n % WRING], 16)
                if ring == "row":
                    _, l, st, r = what
                    if n >= RROWS:
                        sp.wait_ge(rows_used, n - RROWS + 1)
                    if isinstance(r, str):
                        src = t_in["ln"][l, int(r[0]) - 1, "gb".index(r[1])]
                    else:
                        sp.wait_ge(mod_stored[r], 16 * (l + 1))
                        src = mod_dram[l, st, r]
                    sp.dma_start(rows[:, n % RROWS, :], src.partition_broadcast(P)).then_inc(rows_in[n % RROWS], 16)
                if ring == "bias":
                    if what[1] > 0 and what[2] == 0:
                        end = max(i for i, y in enumerate(STEPS) if y[0] == "route" and y[1] == what[1] - 1)
                        sp.wait_ge(mm_free, mm_after[end])
                    if n >= 1:
                        sp.wait_ge(mod_row, n)
                    sp.dma_start(brow[0:2, :], t_in["b_mod"][what[1], what[2]].partition_broadcast(2)
                                 ).then_inc(bias_in, 16)
                if ring == "cache":
                    if n > 0:
                        end = max(i for i, y in enumerate(STEPS) if y[0] == "wout" and y[1] == n - 1 and y[3] == 2 and y[4] == 0)
                        sp.wait_ge(mm_free, mm_after[end])
                    sp.dma_start(cache[:], t_in["cache"][n]).then_inc(cache_in, 16)
            ys = 0
            for b, dst in ((0, t_out["y_prompt"]), (1, t_out["y_sample"][0:P, :]), (2, t_out["y_sample"][P:2 * P, :])):
                ys += 1
                sp.wait_ge(y_ready, ys)
                sp.dma_start(dst, x[:, b, :]).then_inc(y_stored, 16)
            sp.wait_ge(y_stored, 16 * ys)

        @block.gpsimd
        def _(pool):
            blocks_seen = 0
            for (kind, l, s, b, e), mm, t, slot in walk():
                if kind != "peer":
                    continue
                k0, n = e
                if k0 == 0:
                    blocks_seen += 1
                    pool.wait_ge(idx_ready, blocks_seen)
                for k in range(k0, k0 + n):
                    g = slot + k - k0
                    if g >= RING:
                        pool.wait_ge(slot_done, g - RING + 1)
                    pool.indirect_dma_start(expert[:, g % RING, :], None, t_in["experts"],
                                            bass.IndirectOffsetOnAxis(eidx[:, part(l, b), k:k + 1], 0)
                                            ).then_inc(landed[g % RING], 16)

        @block.tensor
        def _(pe):
            n = counter()
            tile = 0

            def mm_bank(u):
                if u >= 2:
                    pe.wait_ge(mm_free, u - 1)
                return mmb[u % 2]

            def t_bank(u):
                if u >= 2:
                    pe.wait_ge(t_free, u - 1)
                return trb[u % 2]

            def weights():
                nonlocal tile
                pe.wait_ge(w_in_slot[tile % WRING], 16 * (tile // WRING + 1))
                tile += 1
                return wt[:, (tile - 1) % WRING, :]

            for (kind, l, s, b, e), mm, t, slot in walk():
                B = BLOCKS.get(s, ())
                NB, KB = len(B), KEYS.get(s, 0)
                K = KB * P
                j = max(b - 1, 0)
                cols = slice(j * P, (j + 1) * P)

                if kind == "cond":
                    pe.wait_ge(cond_silu, 1)
                    pe.transpose(t_bank(t)[:, 0:16], cond_rows, ident[0:16, 0:16]).then_inc(t_full, 1)

                if kind == "mod":
                    if l == 0 and b == 0 and e == 0:
                        pe.wait_ge(t_free, 1)
                    bank = mm_bank(mm)
                    w = weights()
                    for kt in range(KT):
                        m = pe.matmul(bank[0:2, 0:256], csT[:, :, kt], w[:, kt * 256:(kt + 1) * 256],
                                      start=kt == 0, stop=kt == KT - 1)
                    m.then_inc(mm_full, 1)

                if kind == "h_t":
                    if e == 2:
                        pe.wait_ge(h2_ready, n("h2"))
                        src = h2[:, part(l, b), :]
                    else:
                        pe.wait_ge(tok_ready, n("tok"))
                        src = tok[:]
                    for half in range(2):
                        bank = t_bank(t + half)
                        for q in range(4):
                            c = 4 * half + q
                            m = pe.transpose(bank[:, q * P:(q + 1) * P], src[:, c * P:(c + 1) * P], ident[:])
                        m.then_inc(t_full, 1)

                if kind == "win":
                    if b == 0:
                        pe.wait_ge(t_free, t)
                    bank = mm_bank(mm)
                    w = weights()
                    for jj in range(NB):
                        for kt in range(KT):
                            m = pe.matmul(bank[:, jj * 256:jj * 256 + IN_C], hT[:, kt, jj * P:(jj + 1) * P],
                                          w[:, kt * IN_C:(kt + 1) * IN_C], start=kt == 0, stop=kt == KT - 1)
                    m.then_inc(mm_full, 1)

                if kind == "wout":
                    if e == 0:
                        pe.wait_ge(t_free, t)
                    bank = mm_bank(mm)
                    w = weights()
                    for kt in range(KT):
                        m = pe.matmul(bank[:, 0:256], hT[:, kt, cols], w[:, kt * 256:(kt + 1) * 256],
                                      start=kt == 0, stop=kt == KT - 1)
                    m.then_inc(mm_full, 1)

                if kind == "k_t":
                    pe.wait_ge(prep_done, n("prep"))
                    p = proj(b)
                    bank = t_bank(t)
                    for q, c in enumerate((AK, AK + P, GK, CKV)):
                        m = pe.transpose(bank[:, q * P:(q + 1) * P], p[:, c:c + P], ident[:])
                    m.then_inc(t_full, 1)
                    bank = t_bank(t + 1)
                    pe.transpose(bank[0:96, 0:P], p[:, KR - 64:GQ], ident[:]).then_inc(t_full, 1)

                if kind == "q_t":
                    p = proj(b)
                    bank = t_bank(t)
                    for q, c in enumerate((AQ, AQ + P, CQ, CQ + P)):
                        m = pe.transpose(bank[:, q * P:(q + 1) * P], p[:, c:c + P], ident[:])
                    m.then_inc(t_full, 1)
                    bank = t_bank(t + 1)
                    for q in range(4):
                        m = pe.transpose(bank[:, q * P:(q + 1) * P], p[:, GQ + q * P:GQ + (q + 1) * P], ident[:])
                    m.then_inc(t_full, 1)
                    w = weights()
                    bank = mm_bank(mm)
                    pe.wait_ge(t_free, t + 1)
                    for c in range(2):
                        m = pe.matmul(bank[:, 0:UQ_N], cqT[:, c, :], w[:, c * UQ_N:(c + 1) * UQ_N],
                                      start=c == 0, stop=c == 1)
                    m.then_inc(mm_full, 1)

                if kind == "qm_t":
                    if s == "S":
                        pe.wait_ge(roped, n("roped"))
                    else:
                        pe.wait_ge(mm_free, mm)
                    bank = t_bank(t)
                    for h in range(4):
                        m = pe.transpose(bank[0:96, h * P:(h + 1) * P], qm[:, h * 96:(h + 1) * 96], ident[:])
                    m.then_inc(t_full, 1)

                if kind == "cache_t":
                    pe.wait_ge(cache_in, 16 * (l + 1))
                    bank = t_bank(t)
                    for q, c in enumerate((CA_K, CA_K + P, CA_GK, CA_CKV)):
                        m = pe.transpose(bank[:, q * P:(q + 1) * P], cache[:, c:c + P], ident[:])
                    m.then_inc(t_full, 1)
                    bank = t_bank(t + 1)
                    pe.transpose(bank[0:96, 0:P], cache[:, CA_KR - 64:CA_GK], ident[:]).then_inc(t_full, 1)

                if kind == "kv_mla":
                    pe.wait_ge(t_free, t)
                    ukv = weights()[:, 0:UKV_N].rearrange("p (h c) -> p h c", h=4)
                    for h in range(4):
                        bank = mm_bank(mm + h)
                        pe.matmul(bank[0:64, 0:K], ukv[:, h, 0:64], ckvT[:, 0:K], start=True, stop=True
                                  ).then_inc(mm_full, 1)
                    for kb in range(KB):
                        bank = mm_bank(mm + 4 + kb)
                        pe.matmul(bank[:, 0:256], ckvT[:, kb * P:(kb + 1) * P], ukv[:, :, 64:128], start=True, stop=True
                                  ).then_inc(mm_full, 1)

                if kind == "heads":
                    if e == 0:
                        pe.wait_ge(mm_free, mm)
                        pe.wait_ge(t_free, t)
                        at_mm, at_t = {}, {}

                    def scores(m, u):
                        bank = mm_bank(u)
                        if m < 8:
                            r = slice(32 * (m % 4), 32 * (m % 4) + 32)
                            q_, k_ = qdT[r, m // 4, :], kdT[r, m // 4, 0:K]
                        elif m < 12:
                            q_, k_ = qmT[0:96, m - 8, :], kmT[0:96, m - 8, 0:K]
                        else:
                            v = (m - 12) // 4
                            r = slice(64 * v, 64 * v + 64)
                            q_, k_ = qgT[r, (m - 12) % 4, :], kgT[r, 0:K]
                        pe.matmul(bank[:, 0:K], q_, k_, start=True, stop=True).then_inc(sc_full, 1)
                        at_mm[m] = u

                    def turns(m, u):
                        bank = t_bank(u)
                        pe.wait_ge(mm_free, at_mm[m] + 1)
                        for kb in range(KB):
                            tr = pe.transpose(bank[:, kb * P:(kb + 1) * P], E[:, m % 2, kb * P:(kb + 1) * P], ident[:])
                        tr.then_inc(t_full, 1)
                        at_t[m] = u

                    def values(m, kb):
                        own = kb < NB
                        src = proj(B[kb]) if own else cache
                        if m < 8:
                            c = (AV if own else CA_V) + 64 * (m // 2)
                        elif m < 12:
                            return vm[:, kb, 64 * (m - 8):64 * (m - 7)]
                        else:
                            c = (GV if own else CA_GV) + 64 * ((m - 12) // 4)
                        return src[:, c:c + 64]

                    def outputs(m):
                        if m % 8 == 0:
                            use = n("obank") - 1
                            if use >= 2:
                                pe.wait_ge(o_free, use - 1)
                        obank = ob[(n("obank", 0) - 1) % 2]
                        pe.wait_ge(t_free, at_t[m] + 1)
                        for kb in range(KB):
                            o = pe.matmul(obank[:, (m % 8) * 64:(m % 8) * 64 + 64],
                                          ET[:, m % 2, kb * P:(kb + 1) * P], values(m, kb),
                                          start=kb == 0, stop=kb == KB - 1)
                        if m % 8 == 7 or m == MATS - 1:
                            o.then_inc(o_full, 1)

                    turned = t
                    for i in range(PER_STEP):
                        m = e * PER_STEP + i
                        scores(m, mm + i)
                        if m >= 1:
                            turns(m - 1, turned)
                            turned += 1
                        if m >= 2:
                            outputs(m - 2)
                    if m == MATS - 1:
                        turns(m, turned)
                        outputs(m - 1)
                        outputs(m)

                if kind == "route":
                    if e == 0:
                        pe.wait_ge(t_free, t)
                        at_wq = {}
                    if e < WQ_T:
                        bank = mm_bank(mm)
                        w = weights()
                        for i in range(2):
                            for kt in range(KT):
                                m = pe.matmul(bank[:, i * P:(i + 1) * P], w[:, kt * 256 + i * P:kt * 256 + (i + 1) * P],
                                              hT[:, kt, cols], start=kt == 0, stop=kt == KT - 1)
                        m.then_inc(mm_full, 1)
                        at_wq[e] = mm, w
                    if e > 0:
                        use, w = at_wq[e - 1]
                        bank = mm_bank(mm + (e < WQ_T))
                        pe.wait_ge(mm_free, use + 1)
                        for i in range(2):
                            m = pe.matmul(bank[:, i * P:(i + 1) * P], qT[:, (e - 1) % 2, i, :],
                                          w[:, 2048 + i * P:2048 + (i + 1) * P], start=True, stop=True)
                        m.then_inc(mm_full, 1)

                if kind == "peer":
                    k0, cnt = e
                    if k0 == 0:
                        opened = n("acc")
                        if opened > 1:
                            pe.wait_ge(acc_read, opened - 1)

                    def add_slot(r, start):
                        for half in range(2):
                            cs = slice(half * 512, half * 512 + 512)
                            m = pe.matmul(acc[:, cs], diag[:, r, :], expert[:, r, D + half * 512:D + half * 512 + 512],
                                          start=start, stop=False, skip_group_check=True)
                        m.then_inc(slot_done, 1)

                    for k, bodies, size in slot_runs(k0, cnt, k0 == 0):
                        g = slot + k - k0
                        if bodies > 1:
                            with pe.Fori(0, bodies) as it:
                                for i in range(size):
                                    pe.wait_ge(diag_ready, it * RING + (g + i + 1))
                                    add_slot((g + i) % RING, False)
                        else:
                            for i in range(size):
                                pe.wait_ge(diag_ready, g + i + 1)
                                add_slot((g + i) % RING, k + i == 0)

        @block.scalar
        def _(act):
            n = counter()

            def link(ins):
                ins.then_inc(a_seq, 1)
                act.wait_ge(a_seq, n("a_seq"))

            def mm_copy(dst, src_of, u):
                act.wait_ge(mm_full, n("mm_full"))
                act.activation(dst, src_of(mmb[u % 2]), ACT.Copy).then_inc(mm_free, 1)

            def t_wait(u):
                act.wait_ge(t_full, n("t_full"))
                return trb[u % 2]

            act.wait_ge(const_in, 16 * N_CONST)
            act.activation(cond_e, cond_rows, ACT.Exp, scale=-1.0).then_inc(cond_exp, 1)
            act.wait_ge(lam_dots, 2 * L)
            act.activation(small[:, 8:8 + 2 * L], small[:, 0:2 * L], ACT.Exp).then_inc(lam_exp, 1)

            for (kind, l, s, b, e), mm, t, slot in walk():
                B = BLOCKS.get(s, ())
                NB, KB = len(B), KEYS.get(s, 0)
                K = KB * P
                j = max(b - 1, 0)
                cols = slice(j * P, (j + 1) * P)

                if kind == "cond":
                    bank = t_wait(t)
                    act.activation(csT[:], bank[:, 0:16].rearrange("p (s c) -> p s c", s=2), ACT.Copy).then_inc(t_free, 1)

                if kind == "mod":
                    if e == 0:
                        k = n("mod") - 1
                        if k >= 1:
                            act.wait_ge(mod_stored[(k - 1) % 6], 16 * ((k - 1) // 6 + 1))
                    mm_copy(mrow[0:2, e * 256:(e + 1) * 256], lambda bk: bk[0:2, 0:256], mm)
                    if e == MOD_T - 1:
                        act.wait_ge(mod_row, n("mod", 0))
                        act.dma_start(mod_dram[l, :, b, :], mrow[0:2, :]).then_inc(mod_stored[b], 16)

                if kind == "h_t":
                    for half in range(2):
                        bank = t_wait(t + half)
                        act.activation(hT[:, 4 * half:4 * half + 4, cols],
                                       bank[:].rearrange("p (a c) -> p a c", a=4), ACT.Copy).then_inc(t_free, 1)

                if kind == "win":
                    if b == 0 and s == "S":
                        act.wait_ge(kv_stored, n("kv_out", 0))
                        for r in range(6):
                            act.wait_ge(mod_stored[r], 16 * (l + 1))
                    dst = wide[:, 0:NB * WIN].rearrange("p (j c) -> p j c", j=NB)[:, :, b * IN_C:(b + 1) * IN_C]
                    mm_copy(dst, lambda bk: bk[:, 0:NB * 256].rearrange("p (j c) -> p j c", j=NB)[:, :, 0:IN_C], mm)

                if kind == "prep" and s == "P":
                    act.wait_ge(prep_done, n("prep_out"))
                    p = proj(b)
                    for name, c0, c1 in (("diff_k", AK, AV), ("diff_v", AV, CQ), ("mla_ckv", CKV, KR),
                                         ("mla_krope", KR, GQ), ("gqa_k", GK, GV), ("gqa_v", GV, WIN)):
                        act.dma_start(t_out[name][l], p[:, c0:c1]).then_inc(kv_stored, 16)
                        n("kv_out", 16)
                if kind == "prep" and s == "S":
                    n("prep_out")

                if kind == "k_t":
                    bank = t_wait(t)
                    act.activation(kdT[:, :, cols], bank[:, 0:256].rearrange("p (a c) -> p a c", a=2), ACT.Copy)
                    act.activation(kgT[:, cols], bank[:, 256:384], ACT.Copy)
                    act.activation(ckvT[:, cols], bank[:, 384:512], ACT.Copy).then_inc(t_free, 1)
                    bank = t_wait(t + 1)
                    for h in range(4):
                        m = act.activation(kmT[64:96, h, cols], bank[64:96, 0:P], ACT.Copy)
                    m.then_inc(t_free, 1)

                if kind == "q_t":
                    bank = t_wait(t)
                    act.activation(qdT, bank[:, 0:256].rearrange("p (a c) -> p a c", a=2), ACT.Copy, scale=SCALE[0])
                    act.activation(cqT, bank[:, 256:512].rearrange("p (a c) -> p a c", a=2), ACT.Copy).then_inc(t_free, 1)
                    bank = t_wait(t + 1)
                    act.activation(qgT, bank[:].rearrange("p (a c) -> p a c", a=4), ACT.Copy, scale=SCALE[-1]
                                   ).then_inc(t_free, 1)
                    mm_copy(qm, lambda bk: bk[:, 0:UQ_N], mm)

                if kind == "qm_t":
                    bank = t_wait(t)
                    act.activation(qmT[0:96], bank[0:96, :].rearrange("p (a c) -> p a c", a=4), ACT.Copy,
                                   scale=SCALE[8]).then_inc(t_free, 1)

                if kind == "cache_t":
                    kc = slice(2 * P, 3 * P)
                    bank = t_wait(t)
                    act.activation(kdT[:, :, kc], bank[:, 0:256].rearrange("p (a c) -> p a c", a=2), ACT.Copy)
                    act.activation(kgT[:, kc], bank[:, 256:384], ACT.Copy)
                    act.activation(ckvT[:, kc], bank[:, 384:512], ACT.Copy).then_inc(t_free, 1)
                    bank = t_wait(t + 1)
                    for h in range(4):
                        m = act.activation(kmT[64:96, h, kc], bank[64:96, 0:P], ACT.Copy)
                    m.then_inc(t_free, 1)

                if kind == "kv_mla":
                    for h in range(4):
                        mm_copy(kmT[0:64, h, 0:K], lambda bk: bk[0:64, 0:K], mm + h)
                    for kb in range(KB):
                        mm_copy(vm[:, kb, :], lambda bk: bk[:, 0:256], mm + 4 + kb)

                if kind == "heads":
                    def turned(m, u):
                        bank = t_wait(u)
                        act.activation(ET[:, m % 2, 0:K], bank[:, 0:K], ACT.Copy).then_inc(t_free, 1)

                    u = t
                    for i in range(PER_STEP):
                        m = e * PER_STEP + i
                        act.wait_ge(nmax_ready, n("nmax"))
                        act.activation(E[:, m % 2, 0:K], mmb[(mm + i) % 2][:, 0:K], ACT.Exp, bias=neg_max[:, m:m + 1],
                                       accum_out=row_sum[:, m:m + 1]).then_inc(mm_free, 1)
                        if m >= 1:
                            turned(m - 1, u)
                            u += 1
                    if m == MATS - 1:
                        turned(m, u)

                if kind == "wout":
                    mm_copy(tok[:, e * 256:(e + 1) * 256], lambda bk: bk[:, 0:256], mm)

                if kind == "route":
                    if e < WQ_T:
                        mm_copy(qT[:, e % 2], lambda bk: bk[:, 0:256].rearrange("p (i c) -> p i c", i=2), mm)
                    if e > 0:
                        head = n("head") - 1
                        if head >= 2:
                            act.wait_ge(topk_done, head - 1)
                        mm_copy(rs[:, (e - 1) % 2], lambda bk: bk[:, 0:256].rearrange("p (i c) -> p i c", i=2),
                                mm + (e < WQ_T))

                if kind == "pick" and e == 1:
                    act.wait_ge(gate_diff, n("gate"))
                    act.activation(gate[:, part(l, b), :], gate[:, part(l, b), :], ACT.Exp).then_inc(gate_exp, 1)

                if kind == "peer":
                    k0, cnt = e
                    for k, bodies, size in slot_runs(k0, cnt, k0 == 0):
                        g = slot + k - k0
                        if bodies > 1:
                            with act.Fori(0, bodies) as it:
                                for i in range(size):
                                    r = (g + i) % RING
                                    act.wait_ge(dot_ready, it * RING + (g + i + 1))
                                    act.activation(acts[:, r:r + 1], dots[:, r:r + 1], ACT.Gelu_apprx_tanh
                                                   ).then_inc(act_ready, 1)
                        else:
                            for i in range(size):
                                r = (g + i) % RING
                                act.wait_ge(dot_ready, g + i + 1)
                                act.activation(acts[:, r:r + 1], dots[:, r:r + 1], ACT.Gelu_apprx_tanh
                                               ).then_inc(act_ready, 1)
            act.wait_ge(kv_stored, n("kv_out", 0))

        @block.vector
        def _(v):
            n = counter()

            def link(ins):
                ins.then_inc(v_seq, 1)
                v.wait_ge(v_seq, n("v_seq"))

            def inv_sqrt(dst, src, scale):
                w = src.shape[-1]
                val, t = newton[:, 0:w], newton[:, 10:10 + w]
                link(v.tensor_scalar(val, src, scale, EPS, ALU.mult, ALU.add))
                link(v.tensor_scalar(t.bitcast(U32), val.bitcast(U32), 1, None, ALU.logical_shift_right))
                link(v.tensor_scalar(dst.bitcast(U32), t.bitcast(U32), -1.0, float(0x5F3759DF), ALU.mult, ALU.add))
                for _ in range(3):
                    link(v.tensor_tensor(t, dst, dst, ALU.mult))
                    link(v.scalar_tensor_tensor(out=t, in0=t, scalar=-0.5, in1=val, op0=ALU.mult, op1=ALU.mult))
                    link(v.scalar_tensor_tensor(out=dst, in0=t, scalar=1.5, in1=dst, op0=ALU.add, op1=ALU.mult))

            def normed(dst, src):
                for c in range(2):
                    link(v.bn_stats(small[:, 16 + 6 * c:22 + 6 * c], src[:, c * 512:(c + 1) * 512]))
                link(v.bn_aggr(small[:, 28:30], small[:, 16:28]))
                inv_sqrt(small[:, 30:31], small[:, 29:30], 1.0)
                link(v.tensor_scalar(dst, src, small[:, 28:29], small[:, 30:31], ALU.subtract, ALU.mult))

            def rms(p, c0, c1, g0, l):
                link(v.tensor_tensor_reduce(t1[:, 0:c1 - c0], p[:, c0:c1], p[:, c0:c1], 1.0, 0.0,
                                            ALU.mult, ALU.add, small[:, 32:33]))
                inv_sqrt(small[:, 33:34], small[:, 32:33], 1.0 / (c1 - c0))
                link(v.scalar_tensor_tensor(out=p[:, c0:c1], in0=p[:, c0:c1], scalar=small[:, 33:34],
                                            in1=gain[:, l, g0:g0 + c1 - c0], op0=ALU.mult, op1=ALU.mult))

            def head_rms(p, heads, gains):
                w = heads * 64
                a = t1[:, 0:w].rearrange("p (h d) -> p h d", d=64)
                p3 = p.rearrange("p (h d) -> p h d", d=64)
                link(v.tensor_tensor(t1[:, 0:w], p, p, ALU.mult))
                link(v.tensor_reduce(small[:, 34:34 + heads], a, X, ALU.add))
                inv_sqrt(small[:, 34:34 + heads], small[:, 34:34 + heads], 1.0 / 64)
                link(v.tensor_tensor(p3, p3, small[:, 34:34 + heads].unsqueeze(2).to_broadcast([P, heads, 64]), ALU.mult))
                for h0, h1, g in gains:
                    link(v.tensor_tensor(p3[:, h0:h1], p3[:, h0:h1], g.unsqueeze(1).to_broadcast([P, h1 - h0, 64]),
                                         ALU.mult))

            def rotate(p3, groups, half, table):
                w = 2 * half
                cos, sin = table[:, 0:w], table[:, w:2 * w]
                a = t1[:, 0:groups * w].rearrange("p (g w) -> p g w", w=w)
                c = t2[:, 0:groups * w].rearrange("p (g w) -> p g w", w=w)
                link(v.tensor_tensor(a, p3, cos.unsqueeze(1).to_broadcast([P, groups, w]), ALU.mult))
                link(v.tensor_tensor(c[:, :, 0:half], p3[:, :, half:w],
                                     sin[:, 0:half].unsqueeze(1).to_broadcast([P, groups, half]), ALU.mult))
                link(v.tensor_tensor(c[:, :, half:w], p3[:, :, 0:half],
                                     sin[:, half:w].unsqueeze(1).to_broadcast([P, groups, half]), ALU.mult))
                link(v.tensor_tensor(p3, a, c, ALU.add))

            def row():
                k = n("row") - 1
                v.wait_ge(rows_in[k % RROWS], 16 * (k // RROWS + 1))
                return rows[:, k % RROWS, :]

            v.wait_ge(const_in, 16 * N_CONST)
            for l in range(L):
                for i in range(2):
                    v.tensor_tensor_reduce(t1[:, 64 * l + 32 * i:64 * l + 32 * i + 32], dlam[:, l, 64 * i:64 * i + 32],
                                           dlam[:, l, 64 * i + 32:64 * i + 64], 1.0, 0.0,
                                           ALU.mult, ALU.add, small[:, 2 * l + i:2 * l + i + 1]).then_inc(lam_dots, 1)
                link(v.tensor_scalar(gain[:, l, G_SUB:G_KV], gain[:, l, G_SUB:G_KV], 1.0 - lambda_init(l), None, ALU.mult))
            v.wait_ge(cond_exp, 1)
            link(v.tensor_scalar(cond_e, cond_e, 1.0, None, ALU.add))
            link(v.reciprocal(cond_e, cond_e))
            v.tensor_tensor(cond_rows, cond_rows, cond_e, ALU.mult).then_inc(cond_silu, 1)
            v.wait_ge(lam_exp, 1)
            for l in range(L):
                link(v.tensor_scalar(neglam[:, l:l + 1], small[:, 9 + 2 * l:10 + 2 * l], small[:, 8 + 2 * l:9 + 2 * l],
                                     -lambda_init(l), ALU.subtract, ALU.add))

            for (kind, l, s, b, e), mm, t, slot in walk():
                B = BLOCKS.get(s, ())
                NB, KB = len(B), KEYS.get(s, 0)
                K = KB * P
                p = proj(b) if kind == "prep" else None

                if kind == "mod" and e == MOD_T - 1:
                    v.wait_ge(bias_in, 16 * n("mod"))
                    v.wait_ge(mm_free, mm + 1)
                    v.scalar_tensor_tensor(out=mrow[0:2, :], in0=mrow[0:2, :], scalar=1.0 if b in (1, 4) else 0.0,
                                           in1=brow[0:2, :], op0=ALU.add, op1=ALU.add).then_inc(mod_row, 1)

                if kind == "ln1":
                    v.wait_ge(t_free, t)
                    normed(tok[:], x[:, b, :])
                    if b == B[0]:
                        gain_row, shift_row = row(), row()
                    link(v.tensor_tensor(tok[:], tok[:], gain_row, ALU.mult))
                    v.tensor_tensor(tok[:], tok[:], shift_row, ALU.add).then_inc(tok_ready, 1)
                    v.wait_ge(tok_ready, n("tok"))
                    if b == B[-1]:
                        v.sem_inc(rows_used, 2)

                if kind == "prep":
                    v.wait_ge(mm_free, mm)
                    rms(p, CQ, CKV, G_CQ, l)
                    rms(p, CKV, KR, G_KV, l)
                    head_rms(p[:, GQ:GV], 10, ((0, 8, gain[:, l, G_Q:G_K]), (8, 10, gain[:, l, G_K:G_SUB])))
                    if s == "S":
                        tb = rope[:, b - 1, :]
                        rotate(p[:, AQ:AV].rearrange("p (g w) -> p g w", w=32), 16, 16, tb[:, 0:64])
                        rotate(p[:, KR:GQ].rearrange("p (g w) -> p g w", w=32), 1, 16, tb[:, 0:64])
                        rotate(p[:, GQ:GV].rearrange("p (g w) -> p g w", w=64), 10, 32, tb[:, 64:192])
                    v.sem_inc(prep_done, 1)

                if kind == "q_rope" and s == "S":
                    v.wait_ge(mm_free, mm)
                    rotate(qm.rearrange("p (h d) -> p h d", d=96)[:, :, 64:96], 4, 16, rope[:, b - 1, 0:64])
                    v.sem_inc(roped, 1)

                if kind == "heads":
                    for i in range(PER_STEP):
                        m = e * PER_STEP + i
                        v.wait_ge(sc_full, n("sc"))
                        v.tensor_reduce(neg_max[:, m:m + 1], mmb[(mm + i) % 2][:, 0:K], X, ALU.max, negate=True
                                        ).then_inc(nmax_ready, 1)
                    for m0 in {2: (0,), 4: (8, 16)}.get(e, ()):
                        use = n("obank") - 1
                        cnt = min(8, MATS - m0)
                        v.wait_ge(o_full, use + 1)
                        link(v.reciprocal(small[:, 46:46 + cnt], row_sum[:, m0:m0 + cnt]))
                        dst = od if m0 == 0 else tok[:, 64 * (m0 - 4):64 * (m0 - 4 + cnt)]
                        v.tensor_tensor(dst.rearrange("p (h d) -> p h d", d=64),
                                        ob[use % 2][:, 0:64 * cnt].rearrange("p (h d) -> p h d", d=64),
                                        small[:, 46:46 + cnt].unsqueeze(2).to_broadcast([P, cnt, 64]),
                                        ALU.mult).then_inc(o_free, 1)
                        v.wait_ge(o_free, use + 1)

                if kind == "mix":
                    pair = od.rearrange("p (h c d) -> p h c d", c=2, d=64)
                    dst = tok[:, 0:256]
                    link(v.scalar_tensor_tensor(out=dst.rearrange("p (h d) -> p h d", d=64), in0=pair[:, :, 1],
                                                scalar=neglam[:, l:l + 1], in1=pair[:, :, 0],
                                                op0=ALU.mult, op1=ALU.add))
                    head_rms(dst, 4, ((0, 4, gain[:, l, G_SUB:G_KV]),))
                    v.sem_inc(tok_ready, 1)
                    n("tok")

                if kind == "ln_x":
                    v.wait_ge(mm_free, mm)
                    y = tok[:]
                    link(v.tensor_tensor(y, y, row(), ALU.mult))
                    link(v.scalar_tensor_tensor(out=y, in0=x[:, b, :], scalar=ALPHA, in1=y, op0=ALU.mult, op1=ALU.add))
                    normed(y, y)
                    link(v.tensor_tensor(y, y, row(), ALU.mult))
                    link(v.tensor_tensor(x[:, b, :], y, row(), ALU.add))
                    v.sem_inc(rows_used, 3)

                if kind == "ln_h":
                    h = h2[:, part(l, b), :]
                    normed(h, x[:, b, :])
                    link(v.tensor_tensor(h, h, row(), ALU.mult))
                    link(v.tensor_tensor(h, h, row(), ALU.add))
                    v.sem_inc(h2_ready, 1)
                    v.sem_inc(rows_used, 2)

                if kind == "route" and e > 0:
                    v.wait_ge(mm_free, mm + (e < WQ_T) + 1)
                    h = e - 1
                    halves = [(i, 2 * h + i, rs[:, h % 2, i, :]) for i in range(2)]
                    for i, c, sc in halves:
                        m = v.max(v16[:, c, 0:8], sc)
                    link(m)
                    for i, c, sc in halves:
                        v.max_index(i16[:, c, 0:8], v16[:, c, 0:8], sc)
                        m = v.match_replace(rep[:, i, :], v16[:, c, 0:8], sc, -3e38)
                    link(m)
                    v.sem_inc(topk_done, 1)
                    for i, c, sc in halves:
                        m = v.max(v16[:, c, 8:16], rep[:, i, :])
                    link(m)
                    for i, c, sc in halves:
                        v.max_index(i16[:, c, 8:16], v16[:, c, 8:16], rep[:, i, :])
                    flat = cand.rearrange("p a c -> p (a c)")
                    link(v.tensor_tensor(cand, v16[:, 2 * h, :].unsqueeze(2).to_broadcast([P, 16, 16]),
                                         v16[:, 2 * h + 1, :].unsqueeze(1).to_broadcast([P, 16, 16]), ALU.add))
                    link(v.max(best[:, h, 0:8], flat))
                    v.max_index(bi[:, h, 0:8], best[:, h, 0:8], flat)
                    link(v.match_replace(cand2, best[:, h, 0:8], flat, -3e38))
                    link(v.max(best[:, h, 8:16], cand2))
                    link(v.max_index(bi[:, h, 8:16], best[:, h, 8:16], cand2))

                if kind == "pick":
                    bflat = bi[:].rearrange("p h k -> p (h k)")
                    if e == 0:
                        v.tensor_copy(i16f, i16[:].rearrange("p (h c) k -> p h c k", c=2))
                        link(v.tensor_scalar(bit[:], bflat, 4, None, ALU.logical_shift_right))
                    else:
                        link(v.tensor_scalar(bit[:], bflat, 15, None, ALU.bitwise_and))
                    link(v.tensor_copy(bf, bit[:]))
                    for h0 in (0, 4):
                        sl = slice(h0 * TOPK, (h0 + 4) * TOPK)
                        link(v.tensor_tensor(eq.rearrange("p h k i -> p (h k) i"),
                                             iota[:].unsqueeze(1).to_broadcast([P, 4 * TOPK, 16]),
                                             bf[:, sl].unsqueeze(2).to_broadcast([P, 4 * TOPK, 16]), ALU.is_equal))
                        link(v.tensor_tensor(eq, eq, i16f[:, h0:h0 + 4, e, :].unsqueeze(2).to_broadcast([P, 4, TOPK, 16]),
                                             ALU.mult))
                        link(v.tensor_reduce((e1, e2)[e][:, sl], eq.rearrange("p h k i -> p (h k) i"), X, ALU.add))
                    if e == 1:
                        g3 = gate[:, part(l, b), :].rearrange("p (h k) -> p h k", h=R_HEADS)
                        v.tensor_tensor(g3, best, best[:, :, 0:1].to_broadcast([P, R_HEADS, TOPK]),
                                        ALU.subtract).then_inc(gate_diff, 1)
                        link(v.tensor_scalar(e1, e1, 128.0, float(l * N_EXP), ALU.mult, ALU.add))
                        link(v.tensor_tensor(eidx[:, part(l, b), :], e1, e2, ALU.add))
                        v.wait_ge(gate_exp, n("gate"))
                        link(v.tensor_reduce(small[:, 54:62], g3, X, ALU.add))
                        link(v.reciprocal(small[:, 54:62], small[:, 54:62]))
                        link(v.tensor_tensor(g3, g3, small[:, 54:62].unsqueeze(2).to_broadcast([P, R_HEADS, TOPK]),
                                             ALU.mult))
                        v.sem_inc(idx_ready, 1)

                if kind == "peer":
                    k0, cnt = e

                    def dot(r):
                        v.tensor_tensor_reduce(expert[:, r, 0:D], expert[:, r, 0:D], h2[:, part(l, b), :], 1.0, 0.0,
                                               ALU.mult, ALU.add, dots[:, r:r + 1]).then_inc(dot_ready, 1)

                    def weigh(r, col):
                        v.tensor_scalar(diag[:, r, :], ident[:], acts[:, r:r + 1], col, ALU.mult, ALU.mult
                                        ).then_inc(diag_ready, 1)

                    for k, bodies, size in slot_runs(k0, cnt, k0 == 0):
                        g = slot + k - k0
                        if bodies > 1:
                            with v.Fori(0, bodies) as it:
                                for i in range(size + 1):
                                    if i < size:
                                        q = g + i
                                        v.wait_ge(landed[q % RING], it * 16 + 16 * (q // RING + 1))
                                        dot(q % RING)
                                    if i > 0:
                                        v.wait_ge(act_ready, it * RING + (g + i))
                                        weigh((g + i - 1) % RING, gate[:, part(l, b), bass.ds(it * RING + (k + i - 1), 1)])
                        else:
                            for i in range(size + 1):
                                if i < size:
                                    q = g + i
                                    v.wait_ge(landed[q % RING], 16 * (q // RING + 1))
                                    dot(q % RING)
                                if i > 0:
                                    v.wait_ge(act_ready, g + i)
                                    weigh((g + i - 1) % RING, gate[:, part(l, b), k + i - 1:k + i])

                if kind == "fin":
                    z = tmp[:, 0:D]
                    r = row()
                    v.wait_ge(slot_done, slot)
                    v.tensor_tensor(z, acc[:], r, ALU.mult).then_inc(acc_read, 1)
                    v.wait_ge(acc_read, n("acc"))
                    link(v.scalar_tensor_tensor(out=z, in0=x[:, b, :], scalar=ALPHA, in1=z, op0=ALU.mult, op1=ALU.add))
                    normed(z, z)
                    link(v.tensor_tensor(z, z, row(), ALU.mult))
                    link(v.tensor_tensor(x[:, b, :], z, row(), ALU.add))
                    v.sem_inc(rows_used, 3)
                    if l == L - 1:
                        v.sem_inc(y_ready, 1)


N_CONST = 9

_OUTS = (("y_prompt", (P, D)), ("y_sample", (2 * P, D)), ("diff_k", (L, P, 256)), ("diff_v", (L, P, 256)),
         ("mla_ckv", (L, P, 128)), ("mla_krope", (L, P, 32)), ("gqa_k", (L, P, 128)), ("gqa_v", (L, P, 128)))


def _tiled(w, width):
    import numpy as np
    layers, rows, cols = w.shape
    v = w.reshape(layers, rows // P, P, cols // width, width)
    return np.ascontiguousarray(v.transpose(0, 3, 2, 1, 4)).reshape(layers, cols // width, P, rows // P * width)


def _rotary():
    import numpy as np
    f = np.float32
    t = np.arange(2 * P)
    out = []
    for dim in (32, 64):
        n = dim // 4
        inv = f(10000.0) ** (-np.arange(n, dtype=f) / f(n))
        ang = np.concatenate([(t // GRID_W).astype(f)[:, None] * inv, (t % GRID_W).astype(f)[:, None] * inv], axis=-1)
        c, s = np.cos(ang), np.sin(ang)
        out += [c, c, -s, s]
    return np.ascontiguousarray(np.concatenate(out, axis=-1).reshape(2, P, 192).transpose(1, 0, 2), dtype=f)


def kernel(x_prompt, x_sample, c, cache_diff_k, cache_diff_v, cache_mla_ckv, cache_mla_krope,
           cache_gqa_k, cache_gqa_v, c_ctx, w_mod, b_mod, w_in, diff_lambda, diff_subln_g,
           mla_q_norm_g, mla_kv_norm_g, mla_w_uq, mla_w_ukv, gqa_q_norm_g, gqa_k_norm_g, w_out,
           ln1_g, ln1_b, ln2_g, ln2_b, peer_wq, peer_keys, peer_u, peer_v):
    import numpy as np
    import concourse.bacc as bacc
    from concourse.bass_utils import run_bass_kernel_spmd

    A = np.asarray
    cat = np.concatenate
    cache = cat([A(a).reshape(L, PAST, -1) for a in (cache_diff_k, cache_diff_v, cache_mla_ckv, cache_mla_krope,
                                                     cache_gqa_k, cache_gqa_v)], axis=-1)
    uq = A(mla_w_uq).reshape(L, 2, P, UQ_N).transpose(0, 2, 1, 3).reshape(L, P, 2 * UQ_N)
    w_in = cat([A(w_in)[:, :, :GQ],
                A(w_in)[:, :, GQ:GK].reshape(L, D, 2, 4, 64).transpose(0, 1, 3, 2, 4).reshape(L, D, 512),
                A(w_in)[:, :, GK:]], axis=-1)
    arrays = {
        "ident": np.eye(P, dtype=np.float32),
        "iota": np.tile(np.arange(TOPK, dtype=np.float32), (P, 1)),
        "rope": _rotary(),
        "cond": cat([A(c_ctx).reshape(KT, P), A(c).reshape(KT, P)]),
        "gain": cat([A(gqa_q_norm_g), A(gqa_k_norm_g), A(diff_subln_g), A(mla_kv_norm_g), A(mla_q_norm_g)], axis=-1),
        "dlam": A(diff_lambda).reshape(L, P),
        "x_prompt": A(x_prompt).reshape(P, D),
        "x_sample": A(x_sample).reshape(2 * P, D),
        "cache": cache,
        "w_mod": _tiled(A(w_mod), 256),
        "b_mod": A(b_mod).reshape(L, 6, D),
        "w_win": _tiled(A(w_in), IN_C),
        "w_uq": uq.reshape(L, 1, P, 2 * UQ_N),
        "w_ukv": A(mla_w_ukv).reshape(L, 1, P, UKV_N),
        "w_wout": _tiled(A(w_out), 256),
        "ln": np.stack([A(ln1_g), A(ln1_b), A(ln2_g), A(ln2_b)], axis=1).reshape(L, 2, 2, D),
        "w_wq": cat([_tiled(A(peer_wq), 256),
                     A(peer_keys).transpose(0, 1, 4, 2, 3).reshape(L, R_HEADS, P, 2 * P)], axis=-1),
        "experts": cat([A(peer_u), A(peer_v)], axis=-1).reshape(L * N_EXP, 2 * D),
    }
    arrays = {k: np.ascontiguousarray(v) for k, v in arrays.items()}
    nc = bacc.Bacc("TRN2", target_bir_lowering=False, num_devices=1)
    t_in = {k: nc.dram_tensor(f"in_{k}", v.shape, F32, kind="ExternalInput").ap() for k, v in arrays.items()}
    t_out = {k: nc.dram_tensor(f"out_{k}", shape, F32, kind="ExternalOutput").ap() for k, shape in _OUTS}
    trunk_program(nc, t_in, t_out)
    r = run_bass_kernel_spmd(nc, [{f"in_{k}": v for k, v in arrays.items()}], core_ids=[0]).results[0]
    o = {k: np.asarray(r[f"out_{k}"]) for k, _ in _OUTS}
    return (o["y_prompt"].reshape(1, P, D), o["y_sample"].reshape(1, 2 * P, D),
            o["diff_k"].reshape(1, L, P, 4, 2, 32), o["diff_v"].reshape(1, L, P, 4, 64),
            o["mla_ckv"].reshape(1, L, P, 128), o["mla_krope"].reshape(1, L, P, 32),
            o["gqa_k"].reshape(1, L, P, 2, 64), o["gqa_v"].reshape(1, L, P, 2, 64))
```

```python
import math
from contextlib import ExitStack

import concourse.bass as bass
from concourse import mybir

F32 = mybir.dt.float32
I32 = mybir.dt.int32
U32 = mybir.dt.uint32
ALU = mybir.AluOpType
ACT = mybir.ActivationFunctionType
X = mybir.AxisListType.X

P = 128
D = 1024
KT = D // P
L = 2
PAST = 128
GRID_W = 64
EPS = 1e-6
ALPHA = (2 * L) ** 0.25
N_EXP = 128 * 128
TOPK = 16
R_HEADS = 8
SLOTS = R_HEADS * TOPK
AQ, AK, AV, CQ, CKV, KR, GQ, GK, GV, WIN = 0, 256, 512, 768, 1024, 1152, 1184, 1696, 1824, 1952
CA_K, CA_V, CA_CKV, CA_KR, CA_GK, CA_GV, CA_N = 0, 256, 512, 640, 672, 800, 928
G_Q, G_K, G_SUB, G_KV, G_CQ, G_N = 0, 64, 128, 192, 320, 576
WT = 2048 + 256
IN_T = 8
IN_C = WIN // IN_T
OUT_T = 4
WQ_T = 8
MOD_T = 4
UQ_N = 384
UKV_N = 512
MATS = 20
SCALE = [32 ** -0.5] * 8 + [96 ** -0.5] * 4 + [64 ** -0.5] * 8
RING = 6
WRING = 3
GELU_C = (2 / math.pi) ** 0.5
RROWS = 4

BLOCKS = {"P": (0,), "S": (1, 2)}
KEYS = {"P": 1, "S": 3}


def lambda_init(l):
    return 0.8 - 0.6 * math.exp(-0.3 * l)


COST = {"mod": 4, "ln1": 3, "win": 7, "prep": 3, "k_t": 2, "q_t": 4, "q_rope": 1, "qm_t": 1, "cache_t": 2,
        "kv_mla": 5, "heads": 2.5, "mix": 3, "h_t": 2, "wout": 4, "ln_x": 3, "ln_h": 3, "route": 6.5, "topk": 2,
        "pick": 3, "fin": 3}
PREP_PIECES = {"P": 2, "S": 4}
HEAD_TURNS = 3


def common_steps(l, s):
    out = []
    for b in BLOCKS[s]:
        out += [("ln1", l, s, b, 0), ("ln1", l, s, b, 1), ("h_t", l, s, b, 0)]
    out += [("win", l, s, n, 0) for n in range(IN_T)]
    for b in BLOCKS[s]:
        out += [("prep", l, s, b, i) for i in range(PREP_PIECES[s])] + [("k_t", l, s, b, 0)]
    if s == "S":
        out += [("cache_t", l, s, 0, 0)]
    return out + [("kv_mla", l, s, 0, 0)]


def block_steps(l, s, b):
    out = [("q_t", l, s, b, 0), ("q_rope", l, s, b, 0), ("qm_t", l, s, b, 0)]
    out += [("heads", l, s, b, i) for i in range(MATS + HEAD_TURNS)]
    out += [("mix", l, s, b, 0), ("h_t", l, s, b, 1)]
    out += [("wout", l, s, b, n) for n in range(OUT_T)]
    out += [("ln_x", l, s, b, i) for i in range(3)] + [("ln_h", l, s, b, i) for i in range(2)] + [("h_t", l, s, b, 2)]
    for n in range(WQ_T + 1):
        out += [("route", l, s, b, n)]
        if n >= 2:
            out += [("topk", l, s, b, n - 2)]
        if n - 2 == R_HEADS // 2 - 1:
            out += [("pick", l, s, b, i) for i in (0, 1)]
    return out + [("topk", l, s, b, R_HEADS - 1)] + [("pick", l, s, b, i) for i in (2, 3)]


def mod_steps(l, rows_=range(6)):
    return [("mod", l, "", row, c) for row in rows_ for c in range(MOD_T)]


def fill(steps, fillers, after):
    out, todo, due = [], list(fillers), 0
    for x in steps:
        out.append(x)
        due += after.get(x[0], 0)
        out += todo[:int(due)]
        todo, due = todo[int(due):], due % 1
    return out + todo


def weave(l, b, steps):
    total = sum(COST[x[0]] for x in steps) or 1
    out, done, cost = [], 0, 0
    for x in steps:
        out.append(x)
        cost += COST[x[0]]
        at = int(SLOTS * cost / total)
        if at > done:
            out.append(("peer", l, "", b, (done, at - done)))
            done = at
    if done < SLOTS:
        out.append(("peer", l, "", b, (done, SLOTS - done)))
    return out + [("fin", l, "", b, 0)]


def fin_rest(l, b):
    return [("fin", l, "", b, i) for i in (1, 2)]


def plan():
    steps = [("cond", 0, "", 0, 0)] + mod_steps(0, (0, 1))
    prompt = common_steps(0, "P") + block_steps(0, "P", 0)
    cut = prompt.index(("pick", 0, "P", 0, 1)) + 1
    between = {"ln1": 1, "prep": 1, "k_t": 1, "q_t": 1, "mix": 2, "ln_x": 1, "ln_h": 1}
    steps += fill(prompt[:cut], mod_steps(0, (2, 3, 4)), between)
    steps += weave(0, 0, prompt[cut:] + mod_steps(0, (5,)) + common_steps(0, "S") + block_steps(0, "S", 1))
    steps += weave(0, 1, fin_rest(0, 0) + block_steps(0, "S", 2) + mod_steps(1, (0, 1)))
    steps += weave(0, 2, fin_rest(0, 1) + fill(common_steps(1, "P") + block_steps(1, "P", 0), mod_steps(1, (2, 3, 4, 5)),
                                               between))
    steps += weave(1, 0, fin_rest(0, 2) + common_steps(1, "S") + block_steps(1, "S", 1))
    steps += weave(1, 1, fin_rest(1, 0) + block_steps(1, "S", 2))
    steps += weave(1, 2, fin_rest(1, 1)) + fin_rest(1, 2)
    return steps


STEPS = plan()


def banks_used(x):
    kind, l, s, i, e = x
    if kind == "heads":
        return int(e < MATS), int(2 <= e < MATS + 2)
    if kind == "route":
        return (e < WQ_T) + (e > 0), 0
    return {"cond": (0, 1), "mod": (1, 0), "h_t": (0, 2), "win": (1, 0), "k_t": (0, 2), "q_t": (1, 2), "qm_t": (0, 1),
            "cache_t": (0, 2), "kv_mla": (4 + KEYS.get(s, 0), 0), "wout": (1, 0)}.get(kind, (0, 0))


def walk():
    mm = t = slot = 0
    for x in STEPS:
        yield x, mm, t, slot
        a, b = banks_used(x)
        mm, t = mm + a, t + b
        if x[0] == "peer":
            slot += x[4][1]


def load_plan():
    at = list(enumerate(STEPS))
    tiles, rows_, biases = [], [], []
    stored = {}
    for i, (kind, l, s, b, e) in at:
        if kind == "mod":
            tiles.append([("mod", l, MOD_T * b + e), i, i])
            if e == 0:
                biases.append([("bias", l, b), i, i])
            if e == MOD_T - 1:
                biases[-1][2] = i
                stored[l, b] = i
        if kind == "win":
            tiles.append([("win", l, b), i, i])
        if kind == "kv_mla":
            tiles.append([("ukv", l, 0), i, i])
        if kind == "q_t":
            tiles.append([("uq", l, 0), i, i])
        if kind == "wout":
            tiles.append([("wout", l, e), i, i])
        if kind == "route" and e < WQ_T:
            tiles.append([("wq", l, e), i, i + 1])
        if kind == "route" and e > 0:
            tiles[-1 - (e < WQ_T)][2] = i
        st = {"P": 0, "S": 1}.get(s, int(b > 0))
        want = {("ln1", 1): (1, 0), ("ln_x", 0): (2,), ("ln_x", 2): ("1g", "1b"), ("ln_h", 1): (4, 3),
                ("fin", 0): (5,), ("fin", 2): ("2g", "2b")}.get((kind, e), ())
        if want and kind == "ln1" and b == 2:
            for r in (-2, -1):
                rows_[r][2] = i
            want = ()
        rows_ += [[("row", l, st, r), i, i] for r in want]
    out = []
    for ring, depth, items in (("tile", WRING, tiles), ("row", RROWS, rows_), ("bias", 1, biases)):
        for n, (what, first, last) in enumerate(items):
            issue = items[n - depth][2] + 1 if n >= depth else 0
            if ring == "row" and not isinstance(what[3], str):
                issue = max(issue, stored[what[1], what[3]] + 1)
            if ring == "bias" and what[1] > 0 and what[2] == 0:
                issue = max(issue, max(i for i, x in at if x[0] == "route" and x[1] == what[1] - 1 and x[3] == 2) + 1)
            assert issue <= first, (what, issue, first)
            out.append((issue, first, ring, n, what))
    for l in range(L):
        ends = [i for i, x in at if x[0] == "heads" and x[1] == l - 1 and x[3] == 2]
        out.append((max(ends) + 2 if ends else 0, max(ends or [0]) + 3, "cache", l, ("cache", l)))
    return sorted(out, key=lambda x: (x[0], x[1])), tiles, rows_


def slot_runs(k, n):
    out = []
    while n and k < 2:
        out.append((k, 1, 1))
        k, n = k + 1, n - 1
    if n // RING >= 2:
        out.append((k, n // RING, RING))
        k, n = k + n // RING * RING, n % RING
    while n:
        m = min(n, RING)
        out.append((k, 1, m))
        k, n = k + m, n - m
    return out


def trunk_program(nc, t_in, t_out):
    with ExitStack() as ctx:
        def sb(name, shape, dt=F32):
            return ctx.enter_context(nc.sbuf_tensor(name, shape, dt))

        def ps(name, shape):
            return ctx.enter_context(nc.psum_tensor(name, shape, F32))

        def sem(name):
            return ctx.enter_context(nc.semaphore(name))

        expert = sb("expert", [P, RING, 2 * D])
        wt = sb("wt", [P, WRING, WT])
        rows = sb("rows", [P, RROWS, D])
        x = sb("x", [P, 3, D])
        h2 = sb("h2", [P, 2, D])
        hT = sb("hT", [P, KT, 2 * P])
        wide = sb("wide", [P, 4096])
        tok = sb("tok", [P, D])
        tmp = sb("tmp", [P, 1280])
        area = sb("area", [P, 7808])
        router = sb("router", [P, 3712])
        cache = sb("cache", [P, CA_N])
        ident = sb("ident", [P, P])
        iota = sb("iota", [P, TOPK])
        rope = sb("rope", [P, 2, 192])
        gain = sb("gain", [P, L, G_N])
        neglam = sb("neglam", [P, L])
        small = sb("small", [P, 64])
        newton = sb("newton", [P, 20])
        neg_max = sb("neg_max", [P, MATS])
        row_sum = sb("row_sum", [P, MATS])
        csT = sb("csT", [P, 2, KT])
        i16 = sb("i16", [P, 16, TOPK], U32)
        bi = sb("bi", [P, R_HEADS, TOPK], U32)
        bit = sb("bit", [P, SLOTS], U32)
        eidx = sb("eidx", [P, 2, SLOTS], I32)
        gate = sb("gate", [P, 2, SLOTS])
        dots = sb("dots", [P, RING])
        acts = sb("acts", [P, RING])
        gelu = sb("gelu", [P, 3, RING])
        diag = sb("diag", [P, RING, P])
        mod_dram = nc.dram_tensor("mod_scratch", (L, 2, 6, D), F32, kind="Internal").ap()

        acc = ps("acc", [P, D])
        mmb = [ps(f"mmb{i}", [P, 512]) for i in range(2)]
        trb = [ps(f"trb{i}", [P, 512]) for i in range(2)]
        ob = [ps(f"ob{i}", [P, 512]) for i in range(2)]

        def cut(t, at, shape):
            n = int(math.prod(shape))
            v = t[:, at:at + n]
            if len(shape) == 2:
                v = v.rearrange("p (a b) -> p a b", b=shape[1])
            if len(shape) == 3:
                v = v.rearrange("p (a b c) -> p a b c", b=shape[1], c=shape[2])
            return v

        def proj(b):
            j = max(b - 1, 0)
            return wide[:, j * WIN:(j + 1) * WIN]

        def part(l, b):
            return (3 * l + b) % 2

        mrow = wide[:, 2 * D:3 * D]
        brow = wide[:, 3 * D:4 * D]
        at = 0
        views = {}
        for name, shape in (("qdT", (2, P)), ("qgT", (4, P)), ("qmT", (4, P)), ("kdT", (2, 384)),
                            ("kgT", (384,)), ("kmT", (4, 384)), ("ckvT", (384,)), ("vm", (3, 256)),
                            ("qm", (UQ_N,)), ("cqT", (2, P)), ("E", (2, 384)), ("ET", (2, 384)), ("od", (512,))):
            views[name] = cut(area, at, shape)
            at += int(math.prod(shape))
        assert at == 7808, at
        qdT, qgT, qmT, kdT, kgT, kmT, ckvT, vm, qm, cqT, E, ET, od = views.values()
        at = 0
        views = {}
        for name, shape in (("qT", (2, 2, P)), ("rs", (2, 2, P)), ("rep", (2, P)), ("cand", (16, 16)), ("cand2", (256,)),
                            ("eq", (4, TOPK, 16)), ("v16", (16, TOPK)), ("i16f", (R_HEADS, 2, TOPK)),
                            ("best", (R_HEADS, TOPK)), ("bf", (SLOTS,)), ("e1", (SLOTS,))):
            views[name] = cut(router, at, shape)
            at += int(math.prod(shape))
        assert at <= 3712, at
        qT, rs, rep, cand, cand2, eq, v16, i16f, best, bf, e1 = views.values()
        e2 = cand2[:, 0:SLOTS]
        dlam = cut(area, 0, (L, P))
        cond_rows = area[0:2 * KT, L * P:L * P + P]
        cond_e = area[0:2 * KT, L * P + P:L * P + 2 * P]
        t1, t2 = tmp[:, 0:640], tmp[:, 640:1280]

        const_in = sem("const_in")
        cache_in = sem("cache_in")
        w_in_slot = [sem(f"w_in_slot{i}") for i in range(WRING)]
        rows_in = [sem(f"rows_in{i}") for i in range(RROWS)]
        rows_used = sem("rows_used")
        bias_in = sem("bias_in")
        mod_row = sem("mod_row")
        mod_stored = [sem(f"mod_stored{i}") for i in range(6)]
        mm_full = sem("mm_full")
        mm_free = sem("mm_free")
        t_full = sem("t_full")
        t_free = sem("t_free")
        sc_full = sem("sc_full")
        nmax_ready = sem("nmax_ready")
        o_full = sem("o_full")
        o_free = sem("o_free")
        lam_dots = sem("lam_dots")
        lam_exp = sem("lam_exp")
        cond_exp = sem("cond_exp")
        cond_silu = sem("cond_silu")
        tok_ready = sem("tok_ready")
        h2_ready = sem("h2_ready")
        prep_done = sem("prep_done")
        roped = sem("roped")
        kv_stored = sem("kv_stored")
        gate_diff = sem("gate_diff")
        gate_exp = sem("gate_exp")
        topk_done = sem("topk_done")
        idx_ready = sem("idx_ready")
        landed = [sem(f"landed{i}") for i in range(RING)]
        dot_ready = sem("dot_ready")
        gelu_step = sem("gelu_step")
        act_ready = sem("act_ready")
        diag_ready = sem("diag_ready")
        slot_done = sem("slot_done")
        acc_read = sem("acc_read")
        y_ready = sem("y_ready")
        y_stored = sem("y_stored")
        v_seq = sem("v_seq")
        a_seq = sem("a_seq")

        def counter():
            seen = {}

            def count(name, n=1):
                seen[name] = seen.get(name, 0) + n
                return seen[name]
            return count

        loads, tile_uses, row_uses = load_plan()
        mm_after = [mm + banks_used(x)[0] for x, mm, _, _ in walk()]

        block = ctx.enter_context(nc.Block())

        @block.sync
        def _(sp):
            for dst, src in ((ident[:], t_in["ident"]), (cond_rows, t_in["cond"]), (iota[:], t_in["iota"]),
                             (rope[:], t_in["rope"]), (gain[:], t_in["gain"].partition_broadcast(P)),
                             (dlam, t_in["dlam"].partition_broadcast(P)),
                             (x[:, 0, :], t_in["x_prompt"]), (x[:, 1, :], t_in["x_sample"][0:P, :]),
                             (x[:, 2, :], t_in["x_sample"][P:2 * P, :])):
                sp.dma_start(dst, src).then_inc(const_in, 16)
            for _, _, ring, n, what in loads:
                if ring == "tile":
                    if n >= WRING:
                        sp.wait_ge(mm_free, mm_after[tile_uses[n - WRING][2]])
                    src = t_in["w_" + what[0]][what[1], what[2]]
                    sp.dma_start(wt[:, n % WRING, 0:src.shape[-1]], src).then_inc(w_in_slot[n % WRING], 16)
                if ring == "row":
                    _, l, st, r = what
                    if n >= RROWS:
                        sp.wait_ge(rows_used, n - RROWS + 1)
                    if isinstance(r, str):
                        src = t_in["ln"][l, int(r[0]) - 1, "gb".index(r[1])]
                    else:
                        sp.wait_ge(mod_stored[r], 16 * (l + 1))
                        src = mod_dram[l, st, r]
                    sp.dma_start(rows[:, n % RROWS, :], src.partition_broadcast(P)).then_inc(rows_in[n % RROWS], 16)
                if ring == "bias":
                    if what[1] > 0 and what[2] == 0:
                        end = max(i for i, y in enumerate(STEPS) if y[0] == "route" and y[1] == what[1] - 1)
                        sp.wait_ge(mm_free, mm_after[end])
                    if n >= 1:
                        sp.wait_ge(mod_row, n)
                    sp.dma_start(brow[0:2, :], t_in["b_mod"][what[1], what[2]].partition_broadcast(2)
                                 ).then_inc(bias_in, 16)
                if ring == "cache":
                    if n > 0:
                        end = max(i for i, y in enumerate(STEPS) if y[0] == "wout" and y[1] == n - 1 and y[3] == 2 and y[4] == 0)
                        sp.wait_ge(mm_free, mm_after[end])
                    sp.dma_start(cache[:], t_in["cache"][n]).then_inc(cache_in, 16)
            ys = 0
            for b, dst in ((0, t_out["y_prompt"]), (1, t_out["y_sample"][0:P, :]), (2, t_out["y_sample"][P:2 * P, :])):
                ys += 1
                sp.wait_ge(y_ready, ys)
                sp.dma_start(dst, x[:, b, :]).then_inc(y_stored, 16)
            sp.wait_ge(y_stored, 16 * ys)

        @block.gpsimd
        def _(pool):
            halves = 0
            for (kind, l, s, b, e), mm, t, slot in walk():
                if kind != "peer":
                    continue
                k0, n = e
                for k in range(k0, k0 + n):
                    g = slot + k - k0
                    if k % (SLOTS // 2) == 0:
                        halves += 1
                        pool.wait_ge(idx_ready, halves)
                    if g >= RING:
                        pool.wait_ge(slot_done, g - RING + 1)
                    pool.indirect_dma_start(expert[:, g % RING, :], None, t_in["experts"],
                                            bass.IndirectOffsetOnAxis(eidx[:, part(l, b), k:k + 1], 0)
                                            ).then_inc(landed[g % RING], 16)

        @block.tensor
        def _(pe):
            n = counter()
            tile = 0

            def mm_bank(u):
                if u >= 2:
                    pe.wait_ge(mm_free, u - 1)
                return mmb[u % 2]

            def t_bank(u):
                if u >= 2:
                    pe.wait_ge(t_free, u - 1)
                return trb[u % 2]

            def weights():
                nonlocal tile
                pe.wait_ge(w_in_slot[tile % WRING], 16 * (tile // WRING + 1))
                tile += 1
                return wt[:, (tile - 1) % WRING, :]

            for (kind, l, s, b, e), mm, t, slot in walk():
                B = BLOCKS.get(s, ())
                NB, KB = len(B), KEYS.get(s, 0)
                K = KB * P
                j = max(b - 1, 0)
                cols = slice(j * P, (j + 1) * P)

                if kind == "cond":
                    pe.wait_ge(cond_silu, 1)
                    pe.transpose(t_bank(t)[:, 0:16], cond_rows, ident[0:16, 0:16]).then_inc(t_full, 1)

                if kind == "mod":
                    if l == 0 and b == 0 and e == 0:
                        pe.wait_ge(t_free, 1)
                    bank = mm_bank(mm)
                    w = weights()
                    for kt in range(KT):
                        m = pe.matmul(bank[0:2, 0:256], csT[:, :, kt], w[:, kt * 256:(kt + 1) * 256],
                                      start=kt == 0, stop=kt == KT - 1)
                    m.then_inc(mm_full, 1)

                if kind == "h_t":
                    if e == 2:
                        pe.wait_ge(h2_ready, n("h2"))
                        src = h2[:, part(l, b), :]
                    else:
                        pe.wait_ge(tok_ready, n("tok"))
                        src = tok[:]
                    for half in range(2):
                        bank = t_bank(t + half)
                        for q in range(4):
                            c = 4 * half + q
                            m = pe.transpose(bank[:, q * P:(q + 1) * P], src[:, c * P:(c + 1) * P], ident[:])
                        m.then_inc(t_full, 1)

                if kind == "win":
                    if b == 0:
                        pe.wait_ge(t_free, t)
                    bank = mm_bank(mm)
                    w = weights()
                    for jj in range(NB):
                        for kt in range(KT):
                            m = pe.matmul(bank[:, jj * 256:jj * 256 + IN_C], hT[:, kt, jj * P:(jj + 1) * P],
                                          w[:, kt * IN_C:(kt + 1) * IN_C], start=kt == 0, stop=kt == KT - 1)
                    m.then_inc(mm_full, 1)

                if kind == "wout":
                    if e == 0:
                        pe.wait_ge(t_free, t)
                    bank = mm_bank(mm)
                    w = weights()
                    for kt in range(KT):
                        m = pe.matmul(bank[:, 0:256], hT[:, kt, cols], w[:, kt * 256:(kt + 1) * 256],
                                      start=kt == 0, stop=kt == KT - 1)
                    m.then_inc(mm_full, 1)

                if kind == "k_t":
                    pe.wait_ge(prep_done, n("prep"))
                    p = proj(b)
                    bank = t_bank(t)
                    for q, c in enumerate((AK, AK + P, GK, CKV)):
                        m = pe.transpose(bank[:, q * P:(q + 1) * P], p[:, c:c + P], ident[:])
                    m.then_inc(t_full, 1)
                    bank = t_bank(t + 1)
                    pe.transpose(bank[0:96, 0:P], p[:, KR - 64:GQ], ident[:]).then_inc(t_full, 1)

                if kind == "q_t":
                    p = proj(b)
                    bank = t_bank(t)
                    for q, c in enumerate((AQ, AQ + P, CQ, CQ + P)):
                        m = pe.transpose(bank[:, q * P:(q + 1) * P], p[:, c:c + P], ident[:])
                    m.then_inc(t_full, 1)
                    bank = t_bank(t + 1)
                    for q in range(4):
                        m = pe.transpose(bank[:, q * P:(q + 1) * P], p[:, GQ + q * P:GQ + (q + 1) * P], ident[:])
                    m.then_inc(t_full, 1)
                    w = weights()
                    bank = mm_bank(mm)
                    pe.wait_ge(t_free, t + 1)
                    for c in range(2):
                        m = pe.matmul(bank[:, 0:UQ_N], cqT[:, c, :], w[:, c * UQ_N:(c + 1) * UQ_N],
                                      start=c == 0, stop=c == 1)
                    m.then_inc(mm_full, 1)

                if kind == "qm_t":
                    if s == "S":
                        pe.wait_ge(roped, n("roped"))
                    else:
                        pe.wait_ge(mm_free, mm)
                    bank = t_bank(t)
                    for h in range(4):
                        m = pe.transpose(bank[0:96, h * P:(h + 1) * P], qm[:, h * 96:(h + 1) * 96], ident[:])
                    m.then_inc(t_full, 1)

                if kind == "cache_t":
                    pe.wait_ge(cache_in, 16 * (l + 1))
                    bank = t_bank(t)
                    for q, c in enumerate((CA_K, CA_K + P, CA_GK, CA_CKV)):
                        m = pe.transpose(bank[:, q * P:(q + 1) * P], cache[:, c:c + P], ident[:])
                    m.then_inc(t_full, 1)
                    bank = t_bank(t + 1)
                    pe.transpose(bank[0:96, 0:P], cache[:, CA_KR - 64:CA_GK], ident[:]).then_inc(t_full, 1)

                if kind == "kv_mla":
                    pe.wait_ge(t_free, t)
                    ukv = weights()[:, 0:UKV_N].rearrange("p (h c) -> p h c", h=4)
                    for h in range(4):
                        bank = mm_bank(mm + h)
                        pe.matmul(bank[0:64, 0:K], ukv[:, h, 0:64], ckvT[:, 0:K], start=True, stop=True
                                  ).then_inc(mm_full, 1)
                    for kb in range(KB):
                        bank = mm_bank(mm + 4 + kb)
                        pe.matmul(bank[:, 0:256], ckvT[:, kb * P:(kb + 1) * P], ukv[:, :, 64:128], start=True, stop=True
                                  ).then_inc(mm_full, 1)

                if kind == "heads":
                    if e == 0:
                        pe.wait_ge(mm_free, mm)
                        pe.wait_ge(t_free, t)
                        at_mm, at_t = {}, {}

                    def scores(m, u):
                        bank = mm_bank(u)
                        if m < 8:
                            r = slice(32 * (m % 4), 32 * (m % 4) + 32)
                            q_, k_ = qdT[r, m // 4, :], kdT[r, m // 4, 0:K]
                        elif m < 12:
                            q_, k_ = qmT[0:96, m - 8, :], kmT[0:96, m - 8, 0:K]
                        else:
                            v = (m - 12) // 4
                            r = slice(64 * v, 64 * v + 64)
                            q_, k_ = qgT[r, (m - 12) % 4, :], kgT[r, 0:K]
                        pe.matmul(bank[:, 0:K], q_, k_, start=True, stop=True).then_inc(sc_full, 1)
                        at_mm[m] = u

                    def turns(m, u):
                        bank = t_bank(u)
                        pe.wait_ge(mm_free, at_mm[m] + 1)
                        for kb in range(KB):
                            tr = pe.transpose(bank[:, kb * P:(kb + 1) * P], E[:, m % 2, kb * P:(kb + 1) * P], ident[:])
                        tr.then_inc(t_full, 1)
                        at_t[m] = u

                    def values(m, kb):
                        own = kb < NB
                        src = proj(B[kb]) if own else cache
                        if m < 8:
                            c = (AV if own else CA_V) + 64 * (m // 2)
                        elif m < 12:
                            return vm[:, kb, 64 * (m - 8):64 * (m - 7)]
                        else:
                            c = (GV if own else CA_GV) + 64 * ((m - 12) // 4)
                        return src[:, c:c + 64]

                    def outputs(m):
                        if m % 8 == 0:
                            use = n("obank") - 1
                            if use >= 2:
                                pe.wait_ge(o_free, use - 1)
                        obank = ob[(n("obank", 0) - 1) % 2]
                        pe.wait_ge(t_free, at_t[m] + 1)
                        for kb in range(KB):
                            o = pe.matmul(obank[:, (m % 8) * 64:(m % 8) * 64 + 64],
                                          ET[:, m % 2, kb * P:(kb + 1) * P], values(m, kb),
                                          start=kb == 0, stop=kb == KB - 1)
                        if m % 8 == 7 or m == MATS - 1:
                            o.then_inc(o_full, 1)

                    if e < MATS:
                        scores(e, mm)
                    if 2 <= e < MATS + 2:
                        turns(e - 2, t)
                    if e >= 3:
                        outputs(e - 3)

                if kind == "route":
                    if e == 0:
                        pe.wait_ge(t_free, t)
                        at_wq = {}
                    if e < WQ_T:
                        bank = mm_bank(mm)
                        w = weights()
                        for i in range(2):
                            for kt in range(KT):
                                m = pe.matmul(bank[:, i * P:(i + 1) * P], w[:, kt * 256 + i * P:kt * 256 + (i + 1) * P],
                                              hT[:, kt, cols], start=kt == 0, stop=kt == KT - 1)
                        m.then_inc(mm_full, 1)
                        at_wq[e] = mm, w
                    if e > 0:
                        use, w = at_wq[e - 1]
                        bank = mm_bank(mm + (e < WQ_T))
                        pe.wait_ge(mm_free, use + 1)
                        for i in range(2):
                            m = pe.matmul(bank[:, i * P:(i + 1) * P], qT[:, (e - 1) % 2, i, :],
                                          w[:, 2048 + i * P:2048 + (i + 1) * P], start=True, stop=True)
                        m.then_inc(mm_full, 1)

                def add_slot(r, start):
                    for half in range(2):
                        cs = slice(half * 512, half * 512 + 512)
                        m = pe.matmul(acc[:, cs], diag[:, r, :], expert[:, r, D + half * 512:D + half * 512 + 512],
                                      start=start, stop=False, skip_group_check=True)
                    m.then_inc(slot_done, 1)

                if kind == "peer":
                    k0, cnt = e
                    for k, bodies, size in slot_runs(k0, cnt):
                        g = slot + k - k0
                        if k == 0:
                            continue
                        if k == 1 and n("acc") > 1:
                            pe.wait_ge(acc_read, n("acc", 0) - 1)
                        if bodies > 1:
                            with pe.Fori(0, bodies) as it:
                                for i in range(size):
                                    pe.wait_ge(diag_ready, it * RING + (g + i))
                                    add_slot((g + i - 1) % RING, False)
                        else:
                            for i in range(size):
                                pe.wait_ge(diag_ready, g + i)
                                add_slot((g + i - 1) % RING, k == 1)

                if kind == "fin" and e == 0:
                    pe.wait_ge(diag_ready, slot)
                    add_slot((slot - 1) % RING, False)

        @block.scalar
        def _(act):
            n = counter()

            def link(ins):
                ins.then_inc(a_seq, 1)
                act.wait_ge(a_seq, n("a_seq"))

            def mm_copy(dst, src_of, u):
                act.wait_ge(mm_full, n("mm_full"))
                act.activation(dst, src_of(mmb[u % 2]), ACT.Copy).then_inc(mm_free, 1)

            def t_wait(u):
                act.wait_ge(t_full, n("t_full"))
                return trb[u % 2]

            act.wait_ge(const_in, 16 * N_CONST)
            act.activation(cond_e, cond_rows, ACT.Exp, scale=-1.0).then_inc(cond_exp, 1)
            act.wait_ge(lam_dots, 2 * L)
            act.activation(small[:, 8:8 + 2 * L], small[:, 0:2 * L], ACT.Exp).then_inc(lam_exp, 1)

            for (kind, l, s, b, e), mm, t, slot in walk():
                B = BLOCKS.get(s, ())
                NB, KB = len(B), KEYS.get(s, 0)
                K = KB * P
                j = max(b - 1, 0)
                cols = slice(j * P, (j + 1) * P)

                if kind == "cond":
                    bank = t_wait(t)
                    act.activation(csT[:], bank[:, 0:16].rearrange("p (s c) -> p s c", s=2), ACT.Copy).then_inc(t_free, 1)

                if kind == "mod":
                    if e == 0:
                        k = n("mod") - 1
                        if k >= 1:
                            act.wait_ge(mod_stored[(k - 1) % 6], 16 * ((k - 1) // 6 + 1))
                    mm_copy(mrow[0:2, e * 256:(e + 1) * 256], lambda bk: bk[0:2, 0:256], mm)
                    if e == MOD_T - 1:
                        act.wait_ge(mod_row, n("mod", 0))
                        act.dma_start(mod_dram[l, :, b, :], mrow[0:2, :]).then_inc(mod_stored[b], 16)

                if kind == "h_t":
                    for half in range(2):
                        bank = t_wait(t + half)
                        act.activation(hT[:, 4 * half:4 * half + 4, cols],
                                       bank[:].rearrange("p (a c) -> p a c", a=4), ACT.Copy).then_inc(t_free, 1)

                if kind == "win":
                    if b == 0 and s == "S":
                        act.wait_ge(kv_stored, n("kv_out", 0))
                        for r in range(6):
                            act.wait_ge(mod_stored[r], 16 * (l + 1))
                    dst = wide[:, 0:NB * WIN].rearrange("p (j c) -> p j c", j=NB)[:, :, b * IN_C:(b + 1) * IN_C]
                    mm_copy(dst, lambda bk: bk[:, 0:NB * 256].rearrange("p (j c) -> p j c", j=NB)[:, :, 0:IN_C], mm)

                if kind == "prep" and e == PREP_PIECES[s] - 1 and s == "P":
                    act.wait_ge(prep_done, n("prep_out"))
                    p = proj(b)
                    for name, c0, c1 in (("diff_k", AK, AV), ("diff_v", AV, CQ), ("mla_ckv", CKV, KR),
                                         ("mla_krope", KR, GQ), ("gqa_k", GK, GV), ("gqa_v", GV, WIN)):
                        act.dma_start(t_out[name][l], p[:, c0:c1]).then_inc(kv_stored, 16)
                        n("kv_out", 16)
                if kind == "prep" and e == PREP_PIECES[s] - 1 and s == "S":
                    n("prep_out")

                if kind == "k_t":
                    bank = t_wait(t)
                    act.activation(kdT[:, :, cols], bank[:, 0:256].rearrange("p (a c) -> p a c", a=2), ACT.Copy)
                    act.activation(kgT[:, cols], bank[:, 256:384], ACT.Copy)
                    act.activation(ckvT[:, cols], bank[:, 384:512], ACT.Copy).then_inc(t_free, 1)
                    bank = t_wait(t + 1)
                    for h in range(4):
                        m = act.activation(kmT[64:96, h, cols], bank[64:96, 0:P], ACT.Copy)
                    m.then_inc(t_free, 1)

                if kind == "q_t":
                    bank = t_wait(t)
                    act.activation(qdT, bank[:, 0:256].rearrange("p (a c) -> p a c", a=2), ACT.Copy, scale=SCALE[0])
                    act.activation(cqT, bank[:, 256:512].rearrange("p (a c) -> p a c", a=2), ACT.Copy).then_inc(t_free, 1)
                    bank = t_wait(t + 1)
                    act.activation(qgT, bank[:].rearrange("p (a c) -> p a c", a=4), ACT.Copy, scale=SCALE[-1]
                                   ).then_inc(t_free, 1)
                    mm_copy(qm, lambda bk: bk[:, 0:UQ_N], mm)

                if kind == "qm_t":
                    bank = t_wait(t)
                    act.activation(qmT[0:96], bank[0:96, :].rearrange("p (a c) -> p a c", a=4), ACT.Copy,
                                   scale=SCALE[8]).then_inc(t_free, 1)

                if kind == "cache_t":
                    kc = slice(2 * P, 3 * P)
                    bank = t_wait(t)
                    act.activation(kdT[:, :, kc], bank[:, 0:256].rearrange("p (a c) -> p a c", a=2), ACT.Copy)
                    act.activation(kgT[:, kc], bank[:, 256:384], ACT.Copy)
                    act.activation(ckvT[:, kc], bank[:, 384:512], ACT.Copy).then_inc(t_free, 1)
                    bank = t_wait(t + 1)
                    for h in range(4):
                        m = act.activation(kmT[64:96, h, kc], bank[64:96, 0:P], ACT.Copy)
                    m.then_inc(t_free, 1)

                if kind == "kv_mla":
                    for h in range(4):
                        mm_copy(kmT[0:64, h, 0:K], lambda bk: bk[0:64, 0:K], mm + h)
                    for kb in range(KB):
                        mm_copy(vm[:, kb, :], lambda bk: bk[:, 0:256], mm + 4 + kb)

                if kind == "heads":
                    def turned(m, u):
                        bank = t_wait(u)
                        act.activation(ET[:, m % 2, 0:K], bank[:, 0:K], ACT.Copy).then_inc(t_free, 1)

                    if e == 0:
                        at_mm = {}
                    at_mm[e] = mm
                    m = e - 1
                    if 0 <= m < MATS:
                        act.wait_ge(nmax_ready, n("nmax"))
                        act.activation(E[:, m % 2, 0:K], mmb[at_mm[m] % 2][:, 0:K], ACT.Exp, bias=neg_max[:, m:m + 1],
                                       accum_out=row_sum[:, m:m + 1]).then_inc(mm_free, 1)
                    if 2 <= e < MATS + 2:
                        turned(e - 2, t)

                if kind == "wout":
                    mm_copy(tok[:, e * 256:(e + 1) * 256], lambda bk: bk[:, 0:256], mm)

                if kind == "route":
                    if e < WQ_T:
                        mm_copy(qT[:, e % 2], lambda bk: bk[:, 0:256].rearrange("p (i c) -> p i c", i=2), mm)
                    if e > 0:
                        head = n("head") - 1
                        if head >= 2:
                            act.wait_ge(topk_done, head - 1)
                        mm_copy(rs[:, (e - 1) % 2], lambda bk: bk[:, 0:256].rearrange("p (i c) -> p i c", i=2),
                                mm + (e < WQ_T))

                if kind == "pick" and e % 2 == 1:
                    act.wait_ge(gate_diff, n("gate"))
                    half = gate[:, part(l, b), e // 2 * SLOTS // 2:(e // 2 + 1) * SLOTS // 2]
                    act.activation(half, half, ACT.Exp).then_inc(gate_exp, 1)

                def activate(r, at):
                    x1, sq, cx, th = dots[:, r:r + 1], gelu[:, 0, r:r + 1], gelu[:, 1, r:r + 1], gelu[:, 2, r:r + 1]
                    act.activation(sq, x1, ACT.Square, scale=(0.044715 * GELU_C) ** 0.5)
                    act.activation(cx, x1, ACT.Copy, scale=GELU_C).then_inc(gelu_step, 1)
                    act.wait_ge(gelu_step, at + 1)
                    act.activation(th, sq, ACT.Tanh, bias=cx, scale=x1).then_inc(gelu_step, 1)
                    act.wait_ge(gelu_step, at + 2)
                    act.activation(acts[:, r:r + 1], th, ACT.Identity, bias=x1, scale=x1).then_inc(act_ready, 1)

                if kind == "peer":
                    k0, cnt = e
                    for k, bodies, size in slot_runs(k0, cnt):
                        g = slot + k - k0
                        if bodies > 1:
                            with act.Fori(0, bodies) as it:
                                for i in range(size):
                                    act.wait_ge(dot_ready, it * RING + (g + i + 1))
                                    activate((g + i) % RING, it * (2 * RING) + 2 * (g + i))
                        else:
                            for i in range(size):
                                act.wait_ge(dot_ready, g + i + 1)
                                activate((g + i) % RING, 2 * (g + i))
            act.wait_ge(kv_stored, n("kv_out", 0))

        @block.vector
        def _(v):
            n = counter()

            def link(ins):
                ins.then_inc(v_seq, 1)
                v.wait_ge(v_seq, n("v_seq"))

            def inv_sqrt(dst, src, scale):
                w = src.shape[-1]
                val, t = newton[:, 0:w], newton[:, 10:10 + w]
                link(v.tensor_scalar(val, src, scale, EPS, ALU.mult, ALU.add))
                link(v.tensor_scalar(t.bitcast(U32), val.bitcast(U32), 1, None, ALU.logical_shift_right))
                link(v.tensor_scalar(dst.bitcast(U32), t.bitcast(U32), -1.0, float(0x5F3759DF), ALU.mult, ALU.add))
                for _ in range(3):
                    link(v.tensor_tensor(t, dst, dst, ALU.mult))
                    link(v.scalar_tensor_tensor(out=t, in0=t, scalar=-0.5, in1=val, op0=ALU.mult, op1=ALU.mult))
                    link(v.scalar_tensor_tensor(out=dst, in0=t, scalar=1.5, in1=dst, op0=ALU.add, op1=ALU.mult))

            def normed(dst, src):
                for c in range(2):
                    link(v.bn_stats(small[:, 16 + 6 * c:22 + 6 * c], src[:, c * 512:(c + 1) * 512]))
                link(v.bn_aggr(small[:, 28:30], small[:, 16:28]))
                inv_sqrt(small[:, 30:31], small[:, 29:30], 1.0)
                link(v.tensor_scalar(dst, src, small[:, 28:29], small[:, 30:31], ALU.subtract, ALU.mult))

            def rms(p, c0, c1, g0, l):
                link(v.tensor_tensor_reduce(t1[:, 0:c1 - c0], p[:, c0:c1], p[:, c0:c1], 1.0, 0.0,
                                            ALU.mult, ALU.add, small[:, 32:33]))
                inv_sqrt(small[:, 33:34], small[:, 32:33], 1.0 / (c1 - c0))
                link(v.scalar_tensor_tensor(out=p[:, c0:c1], in0=p[:, c0:c1], scalar=small[:, 33:34],
                                            in1=gain[:, l, g0:g0 + c1 - c0], op0=ALU.mult, op1=ALU.mult))

            def head_rms(p, heads, gains):
                w = heads * 64
                a = t1[:, 0:w].rearrange("p (h d) -> p h d", d=64)
                p3 = p.rearrange("p (h d) -> p h d", d=64)
                link(v.tensor_tensor(t1[:, 0:w], p, p, ALU.mult))
                link(v.tensor_reduce(small[:, 34:34 + heads], a, X, ALU.add))
                inv_sqrt(small[:, 34:34 + heads], small[:, 34:34 + heads], 1.0 / 64)
                link(v.tensor_tensor(p3, p3, small[:, 34:34 + heads].unsqueeze(2).to_broadcast([P, heads, 64]), ALU.mult))
                for h0, h1, g in gains:
                    link(v.tensor_tensor(p3[:, h0:h1], p3[:, h0:h1], g.unsqueeze(1).to_broadcast([P, h1 - h0, 64]),
                                         ALU.mult))

            def rotate(p3, groups, half, table):
                w = 2 * half
                cos, sin = table[:, 0:w], table[:, w:2 * w]
                a = t1[:, 0:groups * w].rearrange("p (g w) -> p g w", w=w)
                c = t2[:, 0:groups * w].rearrange("p (g w) -> p g w", w=w)
                link(v.tensor_tensor(a, p3, cos.unsqueeze(1).to_broadcast([P, groups, w]), ALU.mult))
                link(v.tensor_tensor(c[:, :, 0:half], p3[:, :, half:w],
                                     sin[:, 0:half].unsqueeze(1).to_broadcast([P, groups, half]), ALU.mult))
                link(v.tensor_tensor(c[:, :, half:w], p3[:, :, 0:half],
                                     sin[:, half:w].unsqueeze(1).to_broadcast([P, groups, half]), ALU.mult))
                link(v.tensor_tensor(p3, a, c, ALU.add))

            def row():
                k = n("row") - 1
                v.wait_ge(rows_in[k % RROWS], 16 * (k // RROWS + 1))
                return rows[:, k % RROWS, :]

            v.wait_ge(const_in, 16 * N_CONST)
            for l in range(L):
                for i in range(2):
                    v.tensor_tensor_reduce(t1[:, 64 * l + 32 * i:64 * l + 32 * i + 32], dlam[:, l, 64 * i:64 * i + 32],
                                           dlam[:, l, 64 * i + 32:64 * i + 64], 1.0, 0.0,
                                           ALU.mult, ALU.add, small[:, 2 * l + i:2 * l + i + 1]).then_inc(lam_dots, 1)
                link(v.tensor_scalar(gain[:, l, G_SUB:G_KV], gain[:, l, G_SUB:G_KV], 1.0 - lambda_init(l), None, ALU.mult))
            v.wait_ge(cond_exp, 1)
            link(v.tensor_scalar(cond_e, cond_e, 1.0, None, ALU.add))
            link(v.reciprocal(cond_e, cond_e))
            v.tensor_tensor(cond_rows, cond_rows, cond_e, ALU.mult).then_inc(cond_silu, 1)
            v.wait_ge(lam_exp, 1)
            for l in range(L):
                link(v.tensor_scalar(neglam[:, l:l + 1], small[:, 9 + 2 * l:10 + 2 * l], small[:, 8 + 2 * l:9 + 2 * l],
                                     -lambda_init(l), ALU.subtract, ALU.add))

            for (kind, l, s, b, e), mm, t, slot in walk():
                B = BLOCKS.get(s, ())
                NB, KB = len(B), KEYS.get(s, 0)
                K = KB * P
                p = proj(b) if kind == "prep" else None

                if kind == "mod" and e == MOD_T - 1:
                    v.wait_ge(bias_in, 16 * n("mod"))
                    v.wait_ge(mm_free, mm + 1)
                    v.scalar_tensor_tensor(out=mrow[0:2, :], in0=mrow[0:2, :], scalar=1.0 if b in (1, 4) else 0.0,
                                           in1=brow[0:2, :], op0=ALU.add, op1=ALU.add).then_inc(mod_row, 1)

                if kind == "ln1" and e == 0:
                    v.wait_ge(t_free, t)
                    normed(tok[:], x[:, b, :])

                if kind == "ln1" and e == 1:
                    if b == B[0]:
                        gain_row, shift_row = row(), row()
                    link(v.tensor_tensor(tok[:], tok[:], gain_row, ALU.mult))
                    v.tensor_tensor(tok[:], tok[:], shift_row, ALU.add).then_inc(tok_ready, 1)
                    v.wait_ge(tok_ready, n("tok"))
                    if b == B[-1]:
                        v.sem_inc(rows_used, 2)

                if kind == "prep":
                    if e == 0:
                        v.wait_ge(mm_free, mm)
                        rms(p, CQ, CKV, G_CQ, l)
                        rms(p, CKV, KR, G_KV, l)
                    if e == 1:
                        head_rms(p[:, GQ:GV], 10, ((0, 8, gain[:, l, G_Q:G_K]), (8, 10, gain[:, l, G_K:G_SUB])))
                    tb = rope[:, max(b - 1, 0), :]
                    if e == 2:
                        rotate(p[:, AQ:AV].rearrange("p (g w) -> p g w", w=32), 16, 16, tb[:, 0:64])
                        rotate(p[:, KR:GQ].rearrange("p (g w) -> p g w", w=32), 1, 16, tb[:, 0:64])
                    if e == 3:
                        rotate(p[:, GQ:GV].rearrange("p (g w) -> p g w", w=64), 10, 32, tb[:, 64:192])
                    if e == PREP_PIECES[s] - 1:
                        v.sem_inc(prep_done, 1)

                if kind == "q_rope" and s == "S":
                    v.wait_ge(mm_free, mm)
                    rotate(qm.rearrange("p (h d) -> p h d", d=96)[:, :, 64:96], 4, 16, rope[:, b - 1, 0:64])
                    v.sem_inc(roped, 1)

                if kind == "heads":
                    if e == 0:
                        at_mm = {}
                    at_mm[e] = mm
                    m = e - 1
                    if 0 <= m < MATS:
                        v.wait_ge(sc_full, n("sc"))
                        v.tensor_reduce(neg_max[:, m:m + 1], mmb[at_mm[m] % 2][:, 0:K], X, ALU.max, negate=True
                                        ).then_inc(nmax_ready, 1)
                    for m0 in {11: (0,), 19: (8,), 22: (16,)}.get(e, ()):
                        use = n("obank") - 1
                        cnt = min(8, MATS - m0)
                        v.wait_ge(o_full, use + 1)
                        link(v.reciprocal(small[:, 46:46 + cnt], row_sum[:, m0:m0 + cnt]))
                        dst = od if m0 == 0 else tok[:, 64 * (m0 - 4):64 * (m0 - 4 + cnt)]
                        v.tensor_tensor(dst.rearrange("p (h d) -> p h d", d=64),
                                        ob[use % 2][:, 0:64 * cnt].rearrange("p (h d) -> p h d", d=64),
                                        small[:, 46:46 + cnt].unsqueeze(2).to_broadcast([P, cnt, 64]),
                                        ALU.mult).then_inc(o_free, 1)
                        v.wait_ge(o_free, use + 1)

                if kind == "mix":
                    pair = od.rearrange("p (h c d) -> p h c d", c=2, d=64)
                    dst = tok[:, 0:256]
                    link(v.scalar_tensor_tensor(out=dst.rearrange("p (h d) -> p h d", d=64), in0=pair[:, :, 1],
                                                scalar=neglam[:, l:l + 1], in1=pair[:, :, 0],
                                                op0=ALU.mult, op1=ALU.add))
                    head_rms(dst, 4, ((0, 4, gain[:, l, G_SUB:G_KV]),))
                    v.sem_inc(tok_ready, 1)
                    n("tok")

                if kind == "ln_x":
                    y = tok[:]
                    if e == 0:
                        v.wait_ge(mm_free, mm)
                        link(v.tensor_tensor(y, y, row(), ALU.mult))
                        link(v.scalar_tensor_tensor(out=y, in0=x[:, b, :], scalar=ALPHA, in1=y,
                                                    op0=ALU.mult, op1=ALU.add))
                        v.sem_inc(rows_used, 1)
                    if e == 1:
                        normed(y, y)
                    if e == 2:
                        link(v.tensor_tensor(y, y, row(), ALU.mult))
                        link(v.tensor_tensor(x[:, b, :], y, row(), ALU.add))
                        v.sem_inc(rows_used, 2)

                if kind == "ln_h":
                    h = h2[:, part(l, b), :]
                    if e == 0:
                        normed(h, x[:, b, :])
                    if e == 1:
                        link(v.tensor_tensor(h, h, row(), ALU.mult))
                        link(v.tensor_tensor(h, h, row(), ALU.add))
                        v.sem_inc(h2_ready, 1)
                        v.sem_inc(rows_used, 2)

                if kind == "route" and e > 0:
                    if e == 1:
                        at_scores = {}
                    at_scores[e - 1] = mm + (e < WQ_T)

                if kind == "topk":
                    v.wait_ge(mm_free, at_scores[e] + 1)
                    halves = [(i, 2 * e + i, rs[:, e % 2, i, :]) for i in range(2)]
                    for i, c, sc in halves:
                        m = v.max(v16[:, c, 0:8], sc)
                    link(m)
                    for i, c, sc in halves:
                        v.max_index(i16[:, c, 0:8], v16[:, c, 0:8], sc)
                        m = v.match_replace(rep[:, i, :], v16[:, c, 0:8], sc, -3e38)
                    link(m)
                    v.sem_inc(topk_done, 1)
                    for i, c, sc in halves:
                        m = v.max(v16[:, c, 8:16], rep[:, i, :])
                    link(m)
                    for i, c, sc in halves:
                        v.max_index(i16[:, c, 8:16], v16[:, c, 8:16], rep[:, i, :])
                    flat = cand.rearrange("p a c -> p (a c)")
                    link(v.tensor_tensor(cand, v16[:, 2 * e, :].unsqueeze(2).to_broadcast([P, 16, 16]),
                                         v16[:, 2 * e + 1, :].unsqueeze(1).to_broadcast([P, 16, 16]), ALU.add))
                    link(v.max(best[:, e, 0:8], flat))
                    v.max_index(bi[:, e, 0:8], best[:, e, 0:8], flat)
                    link(v.match_replace(cand2, best[:, e, 0:8], flat, -3e38))
                    link(v.max(best[:, e, 8:16], cand2))
                    link(v.max_index(bi[:, e, 8:16], best[:, e, 8:16], cand2))

                if kind == "pick":
                    i, nh = e % 2, R_HEADS // 2
                    h0 = e // 2 * nh
                    sl = slice(h0 * TOPK, (h0 + nh) * TOPK)
                    pairs = bi[:, h0:h0 + nh, :].rearrange("p h k -> p (h k)")
                    if i == 0:
                        v.tensor_copy(i16f[:, h0:h0 + nh],
                                      i16[:, 2 * h0:2 * (h0 + nh), :].rearrange("p (h c) k -> p h c k", c=2))
                        link(v.tensor_scalar(bit[:, sl], pairs, 4, None, ALU.logical_shift_right))
                    else:
                        link(v.tensor_scalar(bit[:, sl], pairs, 15, None, ALU.bitwise_and))
                    link(v.tensor_copy(bf[:, sl], bit[:, sl]))
                    link(v.tensor_tensor(eq.rearrange("p h k i -> p (h k) i"),
                                         iota[:].unsqueeze(1).to_broadcast([P, nh * TOPK, 16]),
                                         bf[:, sl].unsqueeze(2).to_broadcast([P, nh * TOPK, 16]), ALU.is_equal))
                    link(v.tensor_tensor(eq, eq, i16f[:, h0:h0 + nh, i, :].unsqueeze(2).to_broadcast([P, nh, TOPK, 16]),
                                         ALU.mult))
                    link(v.tensor_reduce((e1, e2)[i][:, sl], eq.rearrange("p h k i -> p (h k) i"), X, ALU.add))
                    if i == 1:
                        g3 = gate[:, part(l, b), sl].rearrange("p (h k) -> p h k", h=nh)
                        top = best[:, h0:h0 + nh]
                        v.tensor_tensor(g3, top, top[:, :, 0:1].to_broadcast([P, nh, TOPK]), ALU.subtract
                                        ).then_inc(gate_diff, 1)
                        link(v.tensor_scalar(e1[:, sl], e1[:, sl], 128.0, float(l * N_EXP), ALU.mult, ALU.add))
                        link(v.tensor_tensor(eidx[:, part(l, b), sl], e1[:, sl], e2[:, sl], ALU.add))
                        sums = small[:, 54:54 + nh]
                        v.wait_ge(gate_exp, n("gate"))
                        link(v.tensor_reduce(sums, g3, X, ALU.add))
                        link(v.reciprocal(sums, sums))
                        link(v.scalar_tensor_tensor(out=g3, in0=g3, scalar=0.5,
                                                    in1=sums.unsqueeze(2).to_broadcast([P, nh, TOPK]),
                                                    op0=ALU.mult, op1=ALU.mult))
                        v.sem_inc(idx_ready, 1)

                def dot(r):
                    v.tensor_tensor_reduce(expert[:, r, 0:D], expert[:, r, 0:D], h2[:, part(l, b), :], 1.0, 0.0,
                                           ALU.mult, ALU.add, dots[:, r:r + 1]).then_inc(dot_ready, 1)

                def weigh(r, col):
                    v.tensor_scalar(diag[:, r, :], ident[:], acts[:, r:r + 1], col, ALU.mult, ALU.mult
                                    ).then_inc(diag_ready, 1)

                if kind == "peer":
                    k0, cnt = e
                    for k, bodies, size in slot_runs(k0, cnt):
                        g = slot + k - k0
                        if bodies > 1:
                            with v.Fori(0, bodies) as it:
                                for i in range(size):
                                    q = g + i
                                    v.wait_ge(landed[q % RING], it * 16 + 16 * (q // RING + 1))
                                    dot(q % RING)
                                    v.wait_ge(act_ready, it * RING + q)
                                    weigh((q - 1) % RING, gate[:, part(l, b), bass.ds(it * RING + (k + i - 1), 1)])
                        else:
                            for i in range(size):
                                q = g + i
                                v.wait_ge(landed[q % RING], 16 * (q // RING + 1))
                                dot(q % RING)
                                if k > 0:
                                    v.wait_ge(act_ready, q)
                                    weigh((q - 1) % RING, gate[:, part(l, b), k + i - 1:k + i])

                if kind == "fin":
                    z = tmp[:, 0:D]
                    if e == 0:
                        v.wait_ge(act_ready, slot)
                        weigh((slot - 1) % RING, gate[:, part(l, b), SLOTS - 1:SLOTS])
                        r = row()
                        v.wait_ge(slot_done, slot)
                        v.tensor_tensor(z, acc[:], r, ALU.mult).then_inc(acc_read, 1)
                        v.wait_ge(acc_read, n("acc"))
                        v.sem_inc(rows_used, 1)
                    if e == 1:
                        link(v.scalar_tensor_tensor(out=z, in0=x[:, b, :], scalar=ALPHA, in1=z,
                                                    op0=ALU.mult, op1=ALU.add))
                        normed(z, z)
                    if e == 2:
                        link(v.tensor_tensor(z, z, row(), ALU.mult))
                        link(v.tensor_tensor(x[:, b, :], z, row(), ALU.add))
                        v.sem_inc(rows_used, 2)
                        if l == L - 1:
                            v.sem_inc(y_ready, 1)


N_CONST = 9

_OUTS = (("y_prompt", (P, D)), ("y_sample", (2 * P, D)), ("diff_k", (L, P, 256)), ("diff_v", (L, P, 256)),
         ("mla_ckv", (L, P, 128)), ("mla_krope", (L, P, 32)), ("gqa_k", (L, P, 128)), ("gqa_v", (L, P, 128)))


def _tiled(w, width):
    import numpy as np
    layers, rows, cols = w.shape
    v = w.reshape(layers, rows // P, P, cols // width, width)
    return np.ascontiguousarray(v.transpose(0, 3, 2, 1, 4)).reshape(layers, cols // width, P, rows // P * width)


def _rotary():
    import numpy as np
    f = np.float32
    t = np.arange(2 * P)
    out = []
    for dim in (32, 64):
        n = dim // 4
        inv = f(10000.0) ** (-np.arange(n, dtype=f) / f(n))
        ang = np.concatenate([(t // GRID_W).astype(f)[:, None] * inv, (t % GRID_W).astype(f)[:, None] * inv], axis=-1)
        c, s = np.cos(ang), np.sin(ang)
        out += [c, c, -s, s]
    return np.ascontiguousarray(np.concatenate(out, axis=-1).reshape(2, P, 192).transpose(1, 0, 2), dtype=f)


def kernel(x_prompt, x_sample, c, cache_diff_k, cache_diff_v, cache_mla_ckv, cache_mla_krope,
           cache_gqa_k, cache_gqa_v, c_ctx, w_mod, b_mod, w_in, diff_lambda, diff_subln_g,
           mla_q_norm_g, mla_kv_norm_g, mla_w_uq, mla_w_ukv, gqa_q_norm_g, gqa_k_norm_g, w_out,
           ln1_g, ln1_b, ln2_g, ln2_b, peer_wq, peer_keys, peer_u, peer_v):
    import numpy as np
    import concourse.bacc as bacc
    from concourse.bass_utils import run_bass_kernel_spmd

    A = np.asarray
    cat = np.concatenate
    cache = cat([A(a).reshape(L, PAST, -1) for a in (cache_diff_k, cache_diff_v, cache_mla_ckv, cache_mla_krope,
                                                     cache_gqa_k, cache_gqa_v)], axis=-1)
    uq = A(mla_w_uq).reshape(L, 2, P, UQ_N).transpose(0, 2, 1, 3).reshape(L, P, 2 * UQ_N)
    w_in = cat([A(w_in)[:, :, :GQ],
                A(w_in)[:, :, GQ:GK].reshape(L, D, 2, 4, 64).transpose(0, 1, 3, 2, 4).reshape(L, D, 512),
                A(w_in)[:, :, GK:]], axis=-1)
    arrays = {
        "ident": np.eye(P, dtype=np.float32),
        "iota": np.tile(np.arange(TOPK, dtype=np.float32), (P, 1)),
        "rope": _rotary(),
        "cond": cat([A(c_ctx).reshape(KT, P), A(c).reshape(KT, P)]),
        "gain": cat([A(gqa_q_norm_g), A(gqa_k_norm_g), A(diff_subln_g), A(mla_kv_norm_g), A(mla_q_norm_g)], axis=-1),
        "dlam": A(diff_lambda).reshape(L, P),
        "x_prompt": A(x_prompt).reshape(P, D),
        "x_sample": A(x_sample).reshape(2 * P, D),
        "cache": cache,
        "w_mod": _tiled(A(w_mod), 256),
        "b_mod": A(b_mod).reshape(L, 6, D),
        "w_win": _tiled(A(w_in), IN_C),
        "w_uq": uq.reshape(L, 1, P, 2 * UQ_N),
        "w_ukv": A(mla_w_ukv).reshape(L, 1, P, UKV_N),
        "w_wout": _tiled(A(w_out), 256),
        "ln": np.stack([A(ln1_g), A(ln1_b), A(ln2_g), A(ln2_b)], axis=1).reshape(L, 2, 2, D),
        "w_wq": cat([_tiled(A(peer_wq), 256),
                     A(peer_keys).transpose(0, 1, 4, 2, 3).reshape(L, R_HEADS, P, 2 * P)], axis=-1),
        "experts": cat([A(peer_u), A(peer_v)], axis=-1).reshape(L * N_EXP, 2 * D),
    }
    arrays = {k: np.ascontiguousarray(v) for k, v in arrays.items()}
    nc = bacc.Bacc("TRN2", target_bir_lowering=False, num_devices=1)
    t_in = {k: nc.dram_tensor(f"in_{k}", v.shape, F32, kind="ExternalInput").ap() for k, v in arrays.items()}
    t_out = {k: nc.dram_tensor(f"out_{k}", shape, F32, kind="ExternalOutput").ap() for k, shape in _OUTS}
    trunk_program(nc, t_in, t_out)
    r = run_bass_kernel_spmd(nc, [{f"in_{k}": v for k, v in arrays.items()}], core_ids=[0]).results[0]
    o = {k: np.asarray(r[f"out_{k}"]) for k, _ in _OUTS}
    return (o["y_prompt"].reshape(1, P, D), o["y_sample"].reshape(1, 2 * P, D),
            o["diff_k"].reshape(1, L, P, 4, 2, 32), o["diff_v"].reshape(1, L, P, 4, 64),
            o["mla_ckv"].reshape(1, L, P, 128), o["mla_krope"].reshape(1, L, P, 32),
            o["gqa_k"].reshape(1, L, P, 2, 64), o["gqa_v"].reshape(1, L, P, 2, 64))
```
